# Optimizing a Trainium2 kernel written in Bass

```python
import math
import jax, jax.numpy as jnp
from jax import lax
import numpy as np

D_MODEL = 1024
BATCH = 1
SEQ = 256
DEPTH = 2

N_EVEN = (DEPTH + 1) // 2
N_ODD = DEPTH // 2

DN_ALPHA = (2.0 * DEPTH) ** 0.25
DN_BETA = (8.0 * DEPTH) ** -0.25
LN_EPS = 1e-5

MIX_WIDTH_A = D_MODEL // 2
MIX_WIDTH_B = D_MODEL // 2
CHUNK = 128
GM_GROUPS = 4
GM_GROUP_DIM = MIX_WIDTH_A // GM_GROUPS
DA_HEADS = 4
DA_HEAD_DIM = MIX_WIDTH_B // DA_HEADS // 2
DA_V_DIM = 2 * DA_HEAD_DIM
Q_BLOCK = 128
EVEN_IN = 2 * MIX_WIDTH_A + 3 * MIX_WIDTH_B

RET_HEADS = 4
RET_QK_DIM = D_MODEL // RET_HEADS
RET_V_DIM = 2 * D_MODEL // RET_HEADS
RET_CHUNK = 128
ODD_IN = 2 * D_MODEL + 4 * D_MODEL

D_FF = 7 * D_MODEL // 2
N_EXPERTS = 8
TOP_K = 2

kernel_name = 'hybrid_gmlp_diffattn_retention_moe_deepnorm'

F32 = jnp.float32

def layer_norm(x, g, b):
    xf = x.astype(F32)
    mu = jnp.mean(xf, axis=-1, keepdims=True)
    var = jnp.mean(jnp.square(xf - mu), axis=-1, keepdims=True)
    return ((xf - mu) * lax.rsqrt(var + LN_EPS) * g + b).astype(x.dtype)

def swiglu(x, w1, w3, w2):
    return (jax.nn.silu(x @ w1) * (x @ w3)) @ w2

def chunked_spatial_gating(u, v, w_s, b_s, ln_g, ln_b):
    bsz, s, _ = u.shape
    nc = s // CHUNK
    v = v.reshape(bsz, nc, CHUNK, GM_GROUPS, GM_GROUP_DIM)
    v = layer_norm(v, ln_g, ln_b)
    causal = jnp.tril(jnp.ones((CHUNK, CHUNK), dtype=bool))
    w = jnp.where(causal, w_s, jnp.zeros_like(w_s))
    mixed = jnp.einsum('gts,bcsgd->bctgd', w, v) + b_s.T[None, None, :, :, None]
    return u * mixed.reshape(bsz, s, MIX_WIDTH_A)

def diff_attention(q, k, v, lam_q1, lam_k1, lam_q2, lam_k2, subln_g, layer_idx):
    bsz, s = q.shape[0], q.shape[1]
    lam_init = 0.8 - 0.6 * math.exp(-0.3 * layer_idx)
    lam = (jnp.exp(jnp.sum(lam_q1.astype(F32) * lam_k1.astype(F32)))
           - jnp.exp(jnp.sum(lam_q2.astype(F32) * lam_k2.astype(F32))) + lam_init)
    slopes = 2.0 ** (-8.0 * jnp.arange(1, DA_HEADS + 1, dtype=F32) / DA_HEADS)
    scale = DA_HEAD_DIM ** -0.5
    nb = s // Q_BLOCK
    qb = q.reshape(bsz, nb, Q_BLOCK, DA_HEADS, 2, DA_HEAD_DIM).transpose(1, 0, 2, 3, 4, 5)
    kpos = jnp.arange(s)
    vf = v.astype(F32)

    def block(args):
        i, qi = args
        qpos = i * Q_BLOCK + jnp.arange(Q_BLOCK)
        dist = (qpos[:, None] - kpos[None, :]).astype(F32)
        bias = -slopes[:, None, None] * dist
        scores = jnp.einsum('bqhcd,bkhcd->cbhqk', qi, k, preferred_element_type=F32) * scale + bias
        scores = jnp.where(dist >= 0, scores, -jnp.inf)
        p = jax.nn.softmax(scores, axis=-1)
        attn = p[0] - lam * p[1]
        return jnp.einsum('bhqk,bkhe->bqhe', attn, vf)

    o = lax.map(block, (jnp.arange(nb), qb))
    o = o.transpose(1, 0, 2, 3, 4).reshape(bsz, s, DA_HEADS, DA_V_DIM)
    o = o * lax.rsqrt(jnp.mean(jnp.square(o), axis=-1, keepdims=True) + LN_EPS) * subln_g.astype(F32)
    o = o * (1.0 - lam_init)
    return o.reshape(bsz, s, MIX_WIDTH_B).astype(v.dtype)

def retention(q, k, v):
    bsz, s = q.shape[0], q.shape[1]
    nc = s // RET_CHUNK
    log_g = jnp.log1p(-(2.0 ** (-5.0 - jnp.arange(RET_HEADS, dtype=F32))))
    idx = jnp.arange(RET_CHUNK, dtype=F32)
    rel = idx[:, None] - idx[None, :]
    inner_decay = jnp.where(rel >= 0, jnp.exp(log_g[:, None, None] * jnp.maximum(rel, 0.0)), 0.0)
    q_decay = jnp.exp(log_g[None, :] * (idx[:, None] + 1.0))
    k_decay = jnp.exp(log_g[None, :] * (RET_CHUNK - 1.0 - idx[:, None]))
    chunk_decay = jnp.exp(log_g * RET_CHUNK)

    def to_chunks(t):
        return t.reshape(bsz, nc, RET_CHUNK, RET_HEADS, t.shape[-1]).transpose(1, 0, 2, 3, 4)

    def step(state, xs):
        qc, kc, vc = xs
        scores = jnp.einsum('bqhd,bkhd->bhqk', qc, kc) * inner_decay
        inner = jnp.einsum('bhqk,bkhe->bqhe', scores, vc)
        cross = jnp.einsum('bqhd,bhde->bqhe', qc, state) * q_decay[None, :, :, None]
        new_state = (state * chunk_decay[None, :, None, None]
                     + jnp.einsum('bkhd,bkhe->bhde', kc * k_decay[None, :, :, None], vc))
        return new_state, inner + cross

    state0 = jnp.zeros((bsz, RET_HEADS, RET_QK_DIM, RET_V_DIM), F32)
    _, o = lax.scan(step, state0, (to_chunks(q), to_chunks(k), to_chunks(v)))
    return o.transpose(1, 0, 2, 3, 4).reshape(bsz, s, RET_HEADS, RET_V_DIM)

def even_mixer(x, w_in, w_s, b_s, v_ln_g, v_ln_b, lam_q1, lam_k1, lam_q2, lam_k2, subln_g, w_o, layer_idx):
    bsz, s, _ = x.shape
    h = x @ w_in
    a = MIX_WIDTH_A
    bw = MIX_WIDTH_B
    u, v, q, k, va = jnp.split(h, [a, 2 * a, 2 * a + bw, 2 * a + 2 * bw], axis=-1)
    a_out = chunked_spatial_gating(jax.nn.gelu(u, approximate=False), jax.nn.gelu(v, approximate=False),
                                   w_s, b_s, v_ln_g, v_ln_b)
    q = q.reshape(bsz, s, DA_HEADS, 2, DA_HEAD_DIM)
    k = k.reshape(bsz, s, DA_HEADS, 2, DA_HEAD_DIM)
    va = va.reshape(bsz, s, DA_HEADS, DA_V_DIM)
    b_out = diff_attention(q, k, va, lam_q1, lam_k1, lam_q2, lam_k2, subln_g, layer_idx)
    return jnp.concatenate([a_out, b_out], axis=-1) @ w_o

def odd_mixer(x, w_in, gn_g, w_o):
    bsz, s, _ = x.shape
    h = x @ w_in
    q, k, v, g = jnp.split(h, [D_MODEL, 2 * D_MODEL, 4 * D_MODEL], axis=-1)
    q = q.reshape(bsz, s, RET_HEADS, RET_QK_DIM).astype(F32)
    k = k.reshape(bsz, s, RET_HEADS, RET_QK_DIM).astype(F32) * (RET_QK_DIM ** -0.5)
    v = v.reshape(bsz, s, RET_HEADS, RET_V_DIM).astype(F32)
    o = retention(q, k, v)
    mu = jnp.mean(o, axis=-1, keepdims=True)
    var = jnp.mean(jnp.square(o - mu), axis=-1, keepdims=True)
    o = (o - mu) * lax.rsqrt(var + LN_EPS) * gn_g.astype(F32)
    o = jax.nn.silu(g) * o.reshape(bsz, s, 2 * D_MODEL).astype(x.dtype)
    return o @ w_o

def moe_swiglu(x, w_router, b_router, w1, w3, w2):
    bsz, s, d = x.shape
    xt = x.reshape(-1, d)
    logits = (xt @ w_router).astype(F32) + b_router.astype(F32)
    top_val, top_idx = lax.top_k(logits, TOP_K)
    top_w = jax.nn.softmax(top_val, axis=-1)
    gates = jnp.sum(jax.nn.one_hot(top_idx, N_EXPERTS, dtype=F32) * top_w[..., None], axis=1)
    y = jnp.zeros(xt.shape, F32)
    for e in range(N_EXPERTS):
        y = y + gates[:, e:e + 1] * swiglu(xt, w1[e], w3[e], w2[e])
    return y.astype(x.dtype).reshape(bsz, s, d)

def setup_inputs(seed: int = 0) -> dict:
    key = jax.random.key(seed)
    ks = jax.random.split(key, 32)
    d = D_MODEL

    def nrm(k, shape, scale):
        return jax.random.normal(k, shape, F32) * scale

    def gain(k, shape):
        return 1.0 + 0.05 * jax.random.normal(k, shape, F32)

    return {
        'x': jax.random.normal(ks[0], (BATCH, SEQ, d), F32),
        'even_w_in': nrm(ks[1], (N_EVEN, d, EVEN_IN), d ** -0.5),
        'even_w_s': nrm(ks[2], (N_EVEN, GM_GROUPS, CHUNK, CHUNK), 0.5 * CHUNK ** -0.5),
        'even_b_s': gain(ks[3], (N_EVEN, GM_GROUPS, CHUNK)),
        'even_v_ln_g': gain(ks[4], (N_EVEN, GM_GROUPS, GM_GROUP_DIM)),
        'even_v_ln_b': nrm(ks[5], (N_EVEN, GM_GROUPS, GM_GROUP_DIM), 0.02),
        'even_lam_q1': nrm(ks[6], (N_EVEN, DA_HEAD_DIM), 0.1),
        'even_lam_k1': nrm(ks[7], (N_EVEN, DA_HEAD_DIM), 0.1),
        'even_lam_q2': nrm(ks[8], (N_EVEN, DA_HEAD_DIM), 0.1),
        'even_lam_k2': nrm(ks[9], (N_EVEN, DA_HEAD_DIM), 0.1),
        'even_subln_g': gain(ks[10], (N_EVEN, DA_V_DIM)),
        'even_w_o': nrm(ks[11], (N_EVEN, d, d), DN_BETA * d ** -0.5),
        'even_ln1_g': gain(ks[12], (N_EVEN, d)),
        'even_ln1_b': nrm(ks[13], (N_EVEN, d), 0.02),
        'ffn_w1': nrm(ks[14], (N_EVEN, d, D_FF), d ** -0.5),
        'ffn_w3': nrm(ks[15], (N_EVEN, d, D_FF), d ** -0.5),
        'ffn_w2': nrm(ks[16], (N_EVEN, D_FF, d), DN_BETA * D_FF ** -0.5),
        'even_ln2_g': gain(ks[17], (N_EVEN, d)),
        'even_ln2_b': nrm(ks[18], (N_EVEN, d), 0.02),
        'odd_w_in': nrm(ks[19], (N_ODD, d, ODD_IN), d ** -0.5),
        'odd_gn_g': gain(ks[20], (N_ODD, RET_HEADS, RET_V_DIM)),
        'odd_w_o': nrm(ks[21], (N_ODD, 2 * d, d), DN_BETA * (2 * d) ** -0.5),
        'odd_ln1_g': gain(ks[22], (N_ODD, d)),
        'odd_ln1_b': nrm(ks[23], (N_ODD, d), 0.02),
        'router_w': nrm(ks[24], (N_ODD, d, N_EXPERTS), d ** -0.5),
        'router_b': nrm(ks[25], (N_ODD, N_EXPERTS), 0.01),
        'moe_w1': nrm(ks[26], (N_ODD, N_EXPERTS, d, D_FF), d ** -0.5),
        'moe_w3': nrm(ks[27], (N_ODD, N_EXPERTS, d, D_FF), d ** -0.5),
        'moe_w2': nrm(ks[28], (N_ODD, N_EXPERTS, D_FF, d), DN_BETA * D_FF ** -0.5),
        'odd_ln2_g': gain(ks[29], (N_ODD, d)),
        'odd_ln2_b': nrm(ks[30], (N_ODD, d), 0.02),
    }

def reference(x, even_w_in, even_w_s, even_b_s, even_v_ln_g, even_v_ln_b, even_lam_q1, even_lam_k1,
              even_lam_q2, even_lam_k2, even_subln_g, even_w_o, even_ln1_g, even_ln1_b,
              ffn_w1, ffn_w3, ffn_w2, even_ln2_g, even_ln2_b,
              odd_w_in, odd_gn_g, odd_w_o, odd_ln1_g, odd_ln1_b,
              router_w, router_b, moe_w1, moe_w3, moe_w2, odd_ln2_g, odd_ln2_b):
    for l in range(DEPTH):
        i = l // 2
        if l % 2 == 0:
            mix = even_mixer(x, even_w_in[i], even_w_s[i], even_b_s[i], even_v_ln_g[i], even_v_ln_b[i],
                             even_lam_q1[i], even_lam_k1[i], even_lam_q2[i], even_lam_k2[i],
                             even_subln_g[i], even_w_o[i], l)
            x = layer_norm(DN_ALPHA * x + mix, even_ln1_g[i], even_ln1_b[i])
            x = layer_norm(DN_ALPHA * x + swiglu(x, ffn_w1[i], ffn_w3[i], ffn_w2[i]),
                           even_ln2_g[i], even_ln2_b[i])
        else:
            mix = odd_mixer(x, odd_w_in[i], odd_gn_g[i], odd_w_o[i])
            x = layer_norm(DN_ALPHA * x + mix, odd_ln1_g[i], odd_ln1_b[i])
            x = layer_norm(DN_ALPHA * x + moe_swiglu(x, router_w[i], router_b[i], moe_w1[i], moe_w3[i], moe_w2[i]),
                           odd_ln2_g[i], odd_ln2_b[i])
    return x


_drawn_inputs = setup_inputs


def setup_inputs(seed=0):
    import zlib

    import numpy as np

    out = dict(_drawn_inputs(seed))
    spreads = {}
    factors = {'even_b_s': 6.989,
     'even_v_ln_g': 8.0,
     'even_v_ln_b': 37.641,
     'even_lam_q1': 134.304,
     'even_lam_k1': 2.709,
     'even_lam_k2': 112.025,
     'even_subln_g': 3.411,
     'odd_gn_g': 3.894,
     'router_b': 5.471,
     'odd_ln2_b': 2.773}
    for name, (base, spread) in spreads.items():
        noise = np.random.default_rng([zlib.crc32(name.encode()), seed]).standard_normal(out[name].shape)
        drawn = base * np.exp(spread * noise) if base else spread * noise
        out[name] = __import__('jax').numpy.asarray(drawn.astype(out[name].dtype))
    for name, factor in factors.items():
        out[name] = (out[name] * factor).astype(out[name].dtype)
    return out
```

```python
import math
from contextlib import ExitStack

import numpy as np

import concourse.bass as bass
from concourse import mybir

F32 = mybir.dt.float32
F32R = mybir.dt.float32r
I32 = mybir.dt.int32
ALU = mybir.AluOpType
ACT = mybir.ActivationFunctionType
AX_X = mybir.AxisListType.X

P = 128
SEQ = 256
T = SEQ // P
D = 1024
KB = D // P
DEPTH = 2
ALPHA = (2.0 * DEPTH) ** 0.25
EPS = 1e-5
COLS = 512
PIECE = 2048
FF = 7 * D // 2
STEPS = FF // COLS
FB = COLS // P

GROUPS = 4
HEADS = 4
DH = 64
LAM_INIT = 0.8 - 0.6 * math.exp(0.0)
RET_HEADS = 4
RET_V = 512
EXPERTS = 8
TILES = 2
ITEMS = TILES * EXPERTS
NOT_CHOSEN = 1000.0
LOWEST = -3.0e38

RAW_SLOTS = 6
SPLIT_SLOTS = 3
PIECES_PER_SWIGLU = 6 * STEPS

EVEN_IN = 0
EVEN_OUT = EVEN_IN + 10
FFN = EVEN_OUT + 4
ODD_IN = FFN + PIECES_PER_SWIGLU
ODD_OUT = ODD_IN + 24
MOE = ODD_OUT + 8
EVEN_ORDER = [2, 3, 4, 1, 0]
ODD_CHUNKS = 12
FFN_EVENTS = T * STEPS

TURN_X, TURN_MIX, TURN_X1, TURN_X2, TURN_O, TURN_X3 = 0, 4, 8, 12, 16, 24
TURN_BANKS = ([4, 5, 6, 7] + [2, 3, 6, 7] + [2, 3, 6, 7] + [0, 1, 2, 3]
              + [0, 1, 2, 3, 0, 1, 2, 3] + [2, 3, 5, 6])

C_IDENT, C_PRECEDES, C_ONES, C_SLOT, C_CAUSAL, C_REV, C_ITEM = 0, 128, 256, 384, 512, 640, 648
C_WIDTH = 664
SCORE_COLS = P + SEQ

VEC = dict(ln1=0, ln2=1, gn=2, oln1=3, oln2=4)


def constants():
    table = np.zeros((P, C_WIDTH), np.float32)
    i = np.arange(P)
    table[:, C_IDENT:C_IDENT + P] = np.eye(P)
    table[:, C_PRECEDES:C_PRECEDES + P] = i[:, None] < i[None, :]
    table[:, C_ONES:C_ONES + P] = 1.0
    table[:, C_SLOT:C_SLOT + P] = i[None, :]
    table[:, C_CAUSAL:C_CAUSAL + P] = i[:, None] <= i[None, :]
    table[:, C_REV:C_REV + EXPERTS] = EXPERTS - np.arange(EXPERTS)[None, :]
    table[:, C_ITEM:C_ITEM + ITEMS] = np.arange(ITEMS)[None, :]
    slopes = (2.0 ** (-8.0 * np.arange(1, HEADS + 1) / HEADS)).astype(np.float32)
    q = np.concatenate([np.repeat(i[:, None], P, 1), P + np.repeat(i[:, None], SEQ, 1)], 1)
    k = np.concatenate([np.arange(P), np.arange(SEQ)])[None, :]
    alibi = np.stack([np.where(q >= k, -s * (q - k).astype(np.float32), np.float32(-1e30)) for s in slopes], 1)
    rate = np.log1p(-(2.0 ** (-5.0 - np.arange(RET_HEADS))))
    kk = np.concatenate([np.repeat(i[:, None], SEQ, 1), P + np.repeat(i[:, None], P, 1)], 1)
    qq = np.concatenate([np.arange(SEQ), P + np.arange(P)])[None, :]
    decay = np.stack([np.where(qq >= kk, np.exp(r * np.maximum(qq - kk, 0)) * 256.0 ** -0.5, 0.0) for r in rate], 1)
    return table, alibi.astype(np.float32), decay.astype(np.float32)


def o_block(b):
    return (b + 8) % 16


def plus(base, n):
    return base + n if not (isinstance(base, int) and base == 0) else n


class Chain:

    def __init__(self, eng, sem):
        self.eng, self.sem, self.n = eng, sem, 0

    def link(self, ins):
        self.n += 1
        ins.then_inc(self.sem, 1)
        self.eng.wait_ge(self.sem, self.n)


def hybrid_trunk(nc, a, out):
    with ExitStack() as ctx:
        place = [16512]

        def sb(name, shape, dt=F32, at=None):
            size = 4 * int(np.prod(shape[1:]))
            if at is None:
                at = place[0]
                place[0] += (size + 31) // 32 * 32
            return nc.alloc_sbuf_tensor_at(name, shape, dt, offset=at)

        def region(size):
            at = place[0]
            place[0] += size
            return at

        def sem(name):
            return ctx.enter_context(nc.semaphore(name))

        psum = [ctx.enter_context(nc.psum_tensor(f"bank{i}", [P, COLS], F32)) for i in range(8)]

        raw = sb("raw", [P, RAW_SLOTS, PIECE])
        w_hi = sb("w_hi", [P, SPLIT_SLOTS, PIECE], F32R)
        w_lo = sb("w_lo", [P, SPLIT_SLOTS, PIECE], F32R)
        xt_at = region(2 * 16 * SEQ * 4)
        xt_hi = sb("xt_hi", [P, 16, SEQ], F32R, at=xt_at)
        xt_lo = sb("xt_lo", [P, 16, SEQ], F32R, at=xt_at + 16 * SEQ * 4)
        x = sb("x", [P, T, D])
        table = sb("table", [P, C_WIDTH])
        vec = sb("vec", [P, 2048])
        bias = sb("bias", [P, HEADS, SCORE_COLS])
        ident = table[:, C_IDENT:C_IDENT + P]
        small = sb("small", [P, 160])
        stats = sb("stats", [P, 8, 6])

        upper = xt_at + 8 * SEQ * 4
        v_gain = sb("v_gain", [P, 512], at=upper)
        v_bias = sb("v_bias", [P, 512], at=upper + 2048)
        gate_w = sb("gate_w", [P, GROUPS, P], at=upper + 4096)
        lam_in = sb("lam_in", [P, 4, DH], at=upper + 6144)
        sub_gain = sb("sub_gain", [P, P], at=upper + 7168)
        b_s = sb("b_s", [P, GROUPS], at=upper + 7680)
        work = region(49152)
        mix = sb("mix", [P, T, D], at=work)
        qT = sb("qT", [P, HEADS, SEQ], at=work + 8192)
        kT = sb("kT", [P, HEADS, SEQ], at=work + 12288)
        va = sb("va", [P, T, 512], at=work + 16384)
        u_act = sb("u_act", [P, T, 512], at=work + 20480)
        v_act = sb("v_act", [P, T, 512], at=work + 24576)
        q_nat = sb("q_nat", [P, T, 512], at=work + 28672)
        k_nat = sb("k_nat", [P, T, 512], at=work + 32768)
        prob = sb("prob", [P, 2, 2, SCORE_COLS], at=work + 36864)
        attn = sb("attn", [P, 2, SCORE_COLS], at=work + 43008)
        attnT = sb("attnT", [P, 2, SCORE_COLS], at=work + 46080)
        r_v = sb("r_v", [P, T, 2048], at=work)
        r_g = sb("r_g", [P, T, 2048], at=work + 16384)
        r_qT = sb("r_qT", [P, KB, SEQ], at=work + 32768)
        r_kT = sb("r_kT", [P, KB, SEQ], at=work + 40960)
        qk_nat = sb("qk_nat", [P, 2, T, 512], at=upper)
        spare = region(5120)
        decayed = sb("decayed", [P, 2, SCORE_COLS], at=spare)
        o_norm = sb("o_norm", [P, RET_V], at=spare + 3072)
        silu = sb("silu", [P, T, COLS], at=work)
        g = sb("g", [P, T, COLS], at=work + 4096)
        gT_hi = sb("gT_hi", [P, FB, SEQ], F32R, at=work + 8192)
        gT_lo = sb("gT_lo", [P, FB, SEQ], F32R, at=work + 12288)
        tok_hi = sb("tok_hi", [P, T, D], F32R, at=work + 16384)
        tok_lo = sb("tok_lo", [P, T, D], F32R, at=work + 24576)
        slot_hi = sb("slot_hi", [P, KB, P], F32R, at=work + 32768)
        slot_lo = sb("slot_lo", [P, KB, P], F32R, at=work + 36864)
        y_hi = sb("y_hi", [P, D], F32R, at=work + 40960)
        y_lo = sb("y_lo", [P, D], F32R, at=work + 45056)
        pick = sb("pick", [P, T, P], F32R, at=spare)
        pickT = sb("pickT", [P, SEQ], F32R, at=spare + 1024)
        wr_hi = sb("wr_hi", [P, KB, EXPERTS], F32R, at=spare + 2048)
        wr_lo = sb("wr_lo", [P, KB, EXPERTS], F32R, at=spare + 2304)
        wr = sb("wr", [P, KB, EXPERTS], at=spare + 2560)
        rb = sb("rb", [P, EXPERTS], at=spare + 2816)
        slot_no = sb("slot_no", [P, T, ITEMS], at=spare + 2848)
        gate = sb("gate", [P, T, ITEMS], at=spare + 2976)
        own_slot = sb("own_slot", [P, T, 1])
        plan_f = sb("plan_f", [P, 6, 32], at=spare + 3104)
        plan = sb("plan", [P, 3, ITEMS + 2], I32, at=spare + 3872)
        route = sb("route", [P, 10, T, EXPERTS], at=spare + 4096)
        order = sb("order", [P, ITEMS, ITEMS], at=xt_at)
        plan_g = sb("plan_g", [P, 3, ITEMS + 2], at=xt_at + 1024)
        assert place[0] <= nc.sbuf_usable_end

        def cols(first, n):
            return small[:, first:first + n]

        lam_dot, lam_exp, neg_lam = cols(0, 2), cols(2, 2), cols(4, 1)
        mean_var = small[:, 8:24].rearrange("p (n two) -> p n two", two=2)
        var_eps, std, rstd = cols(24, 8), cols(32, 8), cols(40, 8)
        top, neg_top, total, scale = (small[:, 48 + 8 * i:56 + 8 * i].rearrange("p (b n) -> p b n", b=2)
                                      for i in range(4))
        sub_ss, sub_std = cols(80, 8), cols(88, 8)
        ret_mv = small[:, 96:104].rearrange("p (n two) -> p n two", two=2)
        ret_var, ret_std, ret_rstd = cols(104, 4), cols(108, 4), cols(112, 4)
        peak1, peak2, best, share1, share2, gap, odds = (cols(116 + 2 * i, 2) for i in range(7))

        landed = [sem(f"piece_landed{i}") for i in range(RAW_SLOTS)]
        hi_ready = sem("hi_ready")
        lo_ready = sem("lo_ready")
        piece_used = sem("piece_used")
        x_landed, table_landed, bias_landed = sem("x_landed"), sem("table_landed"), sem("bias_landed")
        gating_landed, decay_landed, router_landed = sem("gating_landed"), sem("decay_landed"), sem("router_landed")
        vec_landed = [sem(f"vec_landed_{n}") for n in VEC]
        x_ready = sem("x_ready")
        turned = sem("turned")
        xt_hi_ready, xt_lo_ready = sem("xt_hi_ready"), sem("xt_lo_ready")
        lin_read = sem("lin_read")
        qk_turned, qT_ready, kT_ready = sem("qk_turned"), sem("qT_ready"), sem("kT_ready")
        scores_done, scores_read = sem("scores_done"), sem("scores_read")
        top_ready, exp_ready = sem("top_ready"), sem("exp_ready")
        attn_ready, attn_turned, attnT_ready = sem("attn_ready"), sem("attn_turned"), sem("attnT_ready")
        pv_done = sem("pv_done")
        lam_dotted, lam_exped = sem("lam_dotted"), sem("lam_exped")
        var_ready, std_ready = sem("var_ready"), sem("std_ready")
        v_ready, gating_done, mix_ready = sem("v_ready"), sem("gating_done"), sem("mix_ready")
        ret_turned, ret_T_ready = sem("ret_turned"), sem("ret_T_ready")
        ret_scores, ret_decayed, ret_out, o_ready = sem("ret_scores"), sem("ret_decayed"), sem("ret_out"), sem("o_ready")
        bias_used = sem("bias_used")
        silu_ready, g_ready, g_turned = sem("silu_ready"), sem("g_ready"), sem("g_turned")
        gT_hi_ready, gT_lo_ready = sem("gT_hi_ready"), sem("gT_lo_ready")
        tok_hi_ready, tok_lo_ready = sem("tok_hi_ready"), sem("tok_lo_ready")
        wr_hi_ready, wr_ready, logits_done = sem("wr_hi_ready"), sem("wr_ready"), sem("logits_done")
        gap_ready, odds_ready = sem("gap_ready"), sem("odds_ready")
        mask_ready, places_done, plan_ready = sem("mask_ready"), sem("places_done"), sem("plan_ready")
        slot_copied, pick_begun = sem("slot_copied"), sem("pick_begun")
        pick_ready, gathered, pick_turned = sem("pick_ready"), sem("gathered"), sem("pick_turned")
        slot_hi_ready, slot_lo_ready, pickT_ready = sem("slot_hi_ready"), sem("slot_lo_ready"), sem("pickT_ready")
        y_hi_ready, y_lo_ready, scattered, added = sem("y_hi_ready"), sem("y_lo_ready"), sem("scattered"), sem("added")
        vector_step = sem("vector_step")
        stored = sem("stored")

        block = ctx.enter_context(nc.Block())

        def col_piece(w, half, first_col):
            return w[half * 4 * P:(half + 1) * 4 * P, bass.ds(first_col, COLS)].rearrange("(k p) n -> p k n", p=P)

        def row_piece(w, pair):
            return w[bass.ds(pair * 2 * P, 2 * P), :].rearrange("(k p) n -> p k n", p=P)

        @block.sync
        def _(sp):
            def load(n, base, src, k, c):
                if not isinstance(base, int) or n >= RAW_SLOTS:
                    sp.wait_ge(lo_ready, plus(base, n + 1 - RAW_SLOTS))
                dst = raw[:, n % RAW_SLOTS, :].rearrange("p (k c) -> p k c", k=k)
                sp.dma_start(dst, src).then_inc(landed[n % RAW_SLOTS], 16)

            def swiglu_stream(n, base, w1, w3, w2):
                def up(n, base, j):
                    for i, w in enumerate((w3, w1)):
                        for half in range(2):
                            load(n + 2 * i + half, base, col_piece(w, half, j * COLS), 4, COLS)

                def down(n, base, j):
                    for half in range(2):
                        load(n + half, base, row_piece(w2, j * 2 + half), 2, D)

                up(n, base, 0)
                with sp.Fori(1, STEPS) as j:
                    here = base + (j - 1) * 6
                    up(n + 4, here, j)
                    down(n + 8, here, j - 1)
                down(n + 4 + 6 * (STEPS - 1), base, STEPS - 1)

            for i, c in enumerate(EVEN_ORDER):
                for half in range(2):
                    load(EVEN_IN + 2 * i + half, 0, col_piece(a["even_w_in"], half, c * COLS), 4, COLS)
            for pair in range(4):
                load(EVEN_OUT + pair, 0, row_piece(a["even_w_o"], pair), 2, D)
            swiglu_stream(FFN, 0, a["ffn_w1"], a["ffn_w3"], a["ffn_w2"])
            for c in range(ODD_CHUNKS):
                for half in range(2):
                    load(ODD_IN + 2 * c + half, 0, col_piece(a["odd_w_in"], half, c * COLS), 4, COLS)
            for pair in range(8):
                load(ODD_OUT + pair, 0, row_piece(a["odd_w_o"], pair), 2, D)

            sp.wait_ge(plan_ready, 1)
            with sp.Fori(0, ITEMS) as k:
                runs = sp.value_load(plan[0:1, 0, bass.ds(k + 1, 1)], min_val=0, max_val=1)
                e = sp.value_load(plan[0:1, 2, bass.ds(k + 1, 1)], min_val=0, max_val=EXPERTS - 1)
                with sp.If(runs > 0):
                    w1, w3, w2 = (a[n][bass.ds(e, 1), :, :].rearrange("o k n -> (o k) n")
                                  for n in ("moe_w1", "moe_w3", "moe_w2"))
                    swiglu_stream(MOE, k * PIECES_PER_SWIGLU, w1, w3, w2)

            for t in range(T):
                sp.wait_ge(x_ready, 3 * T + t + 1)
                sp.dma_start(out[t * P:(t + 1) * P, :], x[:, t, :]).then_inc(stored, 16)
            sp.wait_ge(stored, 16 * T)

        @block.gpsimd
        def _(pool):
            for t in range(T):
                pool.dma_start(x[:, t, :], a["x"][t * P:(t + 1) * P, :]).then_inc(x_landed, 16)
            pool.dma_start(table[:], a["table"]).then_inc(table_landed, 16)
            pool.dma_start(bias[:], a["alibi"]).then_inc(bias_landed, 16)
            for i, n in enumerate(("even_lam_q1", "even_lam_k1", "even_lam_q2", "even_lam_k2")):
                pool.dma_start(lam_in[:, i, :], a[n].partition_broadcast(P)).then_inc(gating_landed, 16)
            pool.dma_start(v_gain[:], a["even_v_ln_g"].partition_broadcast(P)).then_inc(gating_landed, 16)
            pool.dma_start(v_bias[:], a["even_v_ln_b"].partition_broadcast(P)).then_inc(gating_landed, 16)
            pool.dma_start(gate_w[:], a["even_w_s_t"]).then_inc(gating_landed, 16)
            pool.dma_start(b_s[:], a["even_b_s_t"]).then_inc(gating_landed, 16)
            pool.dma_start(sub_gain[:], a["even_subln_g"].partition_broadcast(P)).then_inc(gating_landed, 16)

            def norm_vectors(at, names, width):
                for i, n in enumerate(names):
                    pool.dma_start(vec[:, i * width:(i + 1) * width],
                                   a[n].partition_broadcast(P)).then_inc(vec_landed[at], 16)

            norm_vectors(0, ("even_ln1_g", "even_ln1_b"), D)
            pool.wait_ge(bias_used, 1)
            pool.dma_start(bias[:], a["decay"]).then_inc(decay_landed, 16)
            pool.wait_ge(x_ready, T)
            norm_vectors(1, ("even_ln2_g", "even_ln2_b"), D)
            pool.wait_ge(x_ready, 2 * T)
            norm_vectors(2, ("odd_gn_g",), 2048)
            pool.wait_ge(o_ready, RET_HEADS)
            norm_vectors(3, ("odd_ln1_g", "odd_ln1_b"), D)
            pool.dma_start(wr[:], a["router_w"].rearrange("(k p) e -> p k e", p=P)).then_inc(router_landed, 16)
            pool.dma_start(rb[:], a["router_b"].partition_broadcast(P)).then_inc(router_landed, 16)
            pool.wait_ge(x_ready, 3 * T)
            norm_vectors(4, ("odd_ln2_g", "odd_ln2_b"), D)

            def build_pick(k):
                item = pool.value_load(plan[0:1, 1, bass.ds(k + 1, 1)], min_val=0, max_val=ITEMS - 1)
                pool.tensor_copy(own_slot[:], slot_no[:, :, bass.ds(item, 1)]).then_inc(slot_copied, 1)
                pool.wait_ge(slot_copied, plus(k, 1))
                pool.sem_inc(pick_begun, 1)
                for t in range(T):
                    last = pool.tensor_scalar(pick[:, t, :], table[:, C_SLOT:C_SLOT + P], own_slot[:, t, :],
                                              None, ALU.is_equal)
                last.then_inc(pick_ready, 1)

            pool.wait_ge(plan_ready, 1)
            build_pick(0)
            with pool.Fori(0, ITEMS) as k:
                runs = pool.value_load(plan[0:1, 0, bass.ds(k + 1, 1)], min_val=0, max_val=1)
                with pool.If(runs > 0):
                    pool.wait_ge(pick_turned, k + 1)
                    build_pick(k + 1)

        @block.tensor
        def _(pe):
            def split_product(acc, hi, lo, b_hi, b_lo, start, stop):
                pe.matmul(acc, hi, b_hi, start=start, stop=False)
                pe.matmul(acc, hi, b_lo, start=False, stop=False)
                return pe.matmul(acc, lo, b_hi, start=False, stop=stop)

            def col_product(n, base, half, banks, hi, lo):
                pe.wait_ge(lo_ready, plus(base, n + 1))
                s = n % SPLIT_SLOTS
                for k in range(4):
                    for t, bank in enumerate(banks):
                        last = split_product(psum[bank][:], hi[:, 4 * half + k, t * P:(t + 1) * P],
                                             lo[:, 4 * half + k, t * P:(t + 1) * P],
                                             w_hi[:, s, k * COLS:(k + 1) * COLS], w_lo[:, s, k * COLS:(k + 1) * COLS],
                                             start=(half == 0 and k == 0), stop=(half == 1 and k == 3))
                last.then_inc(piece_used, 1)

            def row_product(n, base, first_block, banks, hi, lo, start, stop):
                pe.wait_ge(lo_ready, plus(base, n + 1))
                s = n % SPLIT_SLOTS
                for k in range(2):
                    for t, pair in enumerate(banks):
                        for h, bank in enumerate(pair):
                            c = k * D + h * COLS
                            last = split_product(psum[bank][:], hi[:, first_block + k, t * P:(t + 1) * P],
                                                 lo[:, first_block + k, t * P:(t + 1) * P],
                                                 w_hi[:, s, c:c + COLS], w_lo[:, s, c:c + COLS],
                                                 start=(start and k == 0), stop=(stop and k == 1))
                last.then_inc(piece_used, 1)

            def turn(group, src, block0):
                bank = psum[TURN_BANKS[group]]
                for k in range(2):
                    for t in range(T):
                        c = (block0 + k) * P
                        last = pe.transpose(bank[:, k * SEQ + t * P:k * SEQ + (t + 1) * P], src[:, t, c:c + P], ident)
                last.then_inc(turned, 1)

            def turn_x(first_group, src=x):
                for i in range(4):
                    turn(first_group + i, src, 2 * i)
                pe.wait_ge(xt_lo_ready, first_group + 4)

            def linear(n, number, banks, hold=2):
                if number >= hold:
                    pe.wait_ge(lin_read, number - hold + 1)
                for half in range(2):
                    col_product(n + half, 0, half, banks, xt_hi, xt_lo)

            def nothing():
                pass

            def swiglu(n, base, events, hi, lo, tiles, y_banks, after_first=nothing, after_turn=nothing,
                       before_last=nothing):
                h3, h1 = [0, 1][:tiles], [2, 3][:tiles] if tiles == 2 else [1]

                def up(n, base, done):
                    for half in range(2):
                        col_product(n + half, base, half, h3, hi, lo)
                    if done is not None:
                        pe.wait_ge(gT_lo_ready, done)
                    for half in range(2):
                        col_product(n + 2 + half, base, half, h1, hi, lo)

                def down(n, base, start, stop):
                    for half in range(2):
                        row_product(n + half, base, 2 * half, y_banks, gT_hi, gT_lo,
                                    start and half == 0, stop and half == 1)

                def turn_g(done):
                    for t in range(tiles):
                        pe.wait_ge(g_ready, plus(done, t + 1))
                        for b in range(FB):
                            last = pe.transpose(psum[h1[t]][:, b * P:(b + 1) * P], g[:, t, b * P:(b + 1) * P], ident)
                        last.then_inc(g_turned, 1)

                up(n, base, None)
                after_first()
                turn_g(events)
                after_turn()
                up(n + 4, base, plus(events, tiles))
                down(n + 8, base, True, False)
                turn_g(plus(events, tiles))
                with pe.Fori(2, STEPS) as j:
                    here = base + (j - 1) * 6
                    now = events + j * tiles
                    up(n + 4, here, now)
                    down(n + 8, here, False, False)
                    turn_g(now)
                before_last()
                pe.wait_ge(gT_lo_ready, plus(events, STEPS * tiles))
                down(n + 4 + 6 * (STEPS - 1), base, False, True)

            pe.wait_ge(table_landed, 16)
            pe.wait_ge(x_landed, 16 * T)
            turn_x(TURN_X)

            linear(EVEN_IN, 0, [0, 1])
            linear(EVEN_IN + 2, 1, [2, 3])
            linear(EVEN_IN + 4, 2, [0, 1])
            pe.wait_ge(lin_read, 2)
            for i, nat in enumerate((q_nat, k_nat)):
                for h in range(HEADS):
                    for t in range(T):
                        c = (h % 2) * SEQ + t * P
                        last = pe.transpose(psum[4 + 2 * i + h // 2][:, c:c + P], nat[:, t, h * P:(h + 1) * P], ident)
                last.then_inc(qk_turned, 1)
            linear(EVEN_IN + 6, 3, [2, 3])

            def scores(h):
                if h >= 2:
                    pe.wait_ge(scores_read, h - 1)
                for c in range(2):
                    bank = psum[4 + 2 * (h % 2) + c]
                    rows = slice(c * DH, (c + 1) * DH)
                    pe.matmul(bank[:, 0:P], qT[rows, h, 0:P], kT[rows, h, 0:P], start=True, stop=True)
                    last = pe.matmul(bank[:, P:SCORE_COLS], qT[rows, h, P:SEQ], kT[rows, h, :], start=True, stop=True)
                last.then_inc(scores_done, 1)

            pe.wait_ge(qT_ready, 1)
            pe.wait_ge(kT_ready, 1)
            scores(0)
            scores(1)
            linear(EVEN_IN + 8, 4, [0, 1])
            scores(2)
            scores(3)

            def turn_attn(h):
                pe.wait_ge(attn_ready, h + 1)
                if h < 2:
                    pe.wait_ge(lin_read, 4)
                for b in range(3):
                    last = pe.transpose(psum[2 + h % 2][:, b * P:(b + 1) * P], attn[:, h % 2, b * P:(b + 1) * P], ident)
                last.then_inc(attn_turned, 1)

            def values(h):
                pe.wait_ge(attnT_ready, h + 1)
                pe.wait_ge(lin_read, 5)
                c = slice(h * P, (h + 1) * P)
                pe.matmul(psum[0][:, c], attnT[:, h % 2, 0:P], va[:, 0, c], start=True, stop=True)
                pe.matmul(psum[1][:, c], attnT[:, h % 2, P:2 * P], va[:, 0, c], start=True, stop=False)
                pe.matmul(psum[1][:, c], attnT[:, h % 2, 2 * P:3 * P], va[:, 1, c],
                          start=False, stop=True).then_inc(pv_done, 1)

            turn_attn(0)
            values(0)
            turn_attn(1)
            values(1)
            pe.wait_ge(v_ready, 1)
            pe.wait_ge(scores_read, 3)
            for t in range(T):
                for gr in range(GROUPS):
                    last = pe.matmul(psum[4 + t][:, gr * P:(gr + 1) * P], gate_w[:, gr, :],
                                     v_act[:, t, gr * P:(gr + 1) * P], start=True, stop=True)
            last.then_inc(gating_done, 1)
            turn_attn(2)
            values(2)
            turn_attn(3)
            values(3)
            pe.wait_ge(mix_ready, 1)
            turn(TURN_MIX, mix, 0)
            turn(TURN_MIX + 1, mix, 2)
            pe.wait_ge(mix_ready, 2)
            turn(TURN_MIX + 2, mix, 4)
            turn(TURN_MIX + 3, mix, 6)
            for pair in range(4):
                pe.wait_ge(xt_lo_ready, TURN_MIX + pair + 1)
                row_product(EVEN_OUT + pair, 0, 2 * pair, [[0, 1], [4, 5]], xt_hi, xt_lo, pair == 0, pair == 3)

            pe.wait_ge(x_ready, T)
            turn_x(TURN_X1)
            swiglu(FFN, 0, 0, xt_hi, xt_lo, T, [[4, 5], [6, 7]])

            pe.wait_ge(x_ready, 2 * T)
            turn_x(TURN_X2)

            def turn_qk(c):
                pe.wait_ge(lin_read, 5 + c + 1)
                if c >= 2:
                    pe.wait_ge(ret_T_ready, c - 1)
                for b in range(4):
                    for t in range(T):
                        k = (b % 2) * SEQ + t * P
                        last = pe.transpose(psum[4 + 2 * (c % 2) + b // 2][:, k:k + P],
                                            qk_nat[:, c % 2, t, b * P:(b + 1) * P], ident)
                last.then_inc(ret_turned, 1)

            def ret_head_scores(h):
                if h:
                    pe.wait_ge(ret_decayed, h)
                for tile, c0, c1 in ((0, 0, SEQ), (1, SEQ, SCORE_COLS)):
                    for k in range(2):
                        last = pe.matmul(psum[4][:, c0:c1], r_kT[:, 2 * h + k, tile * P:(tile + 1) * P],
                                         r_qT[:, 2 * h + k, tile * P:SEQ], start=(k == 0), stop=(k == 1))
                last.then_inc(ret_scores, 1)

            def ret_head_values(h):
                pe.wait_ge(ret_decayed, h + 1)
                if h:
                    pe.wait_ge(o_ready, h)
                s, v = decayed[:, h % 2, :], slice(h * RET_V, (h + 1) * RET_V)
                pe.matmul(psum[5][:], s[:, 0:P], r_v[:, 0, v], start=True, stop=True)
                pe.matmul(psum[6][:], s[:, P:SEQ], r_v[:, 0, v], start=True, stop=False)
                pe.matmul(psum[6][:], s[:, SEQ:SCORE_COLS], r_v[:, 1, v],
                          start=False, stop=True).then_inc(ret_out, 1)

            def turn_o(h):
                pe.wait_ge(o_ready, h + 1)
                for i in range(2):
                    turn(TURN_O + 2 * h + i, r_g, 4 * h + 2 * i)

            for c in range(ODD_CHUNKS):
                if c in (10, 11):
                    pe.wait_ge(xt_lo_ready, TURN_O + 2 * (c - 9))
                linear(ODD_IN + 2 * c, 5 + c, [[0, 1], [2, 3]][c % 2])
                if 1 <= c <= 4:
                    turn_qk(c - 1)
                if c >= 8:
                    h = c - 8
                    if h:
                        turn_o(h - 1)
                    if h == 0:
                        pe.wait_ge(ret_T_ready, 4)
                        pe.wait_ge(lin_read, 5 + 8)
                    ret_head_scores(h)
                    ret_head_values(h)
            odd_banks = [[0, 1], [4, 7]]
            for pair in range(8):
                if pair == 6:
                    pe.wait_ge(lin_read, 5 + ODD_CHUNKS)
                    turn_o(3)
                pe.wait_ge(xt_lo_ready, TURN_O + min(max(pair + 1, 6), 8))
                row_product(ODD_OUT + pair, 0, o_block(2 * pair), odd_banks, xt_hi, xt_lo, pair == 0, pair == 7)

            pe.wait_ge(x_ready, 3 * T)
            turn_x(TURN_X3)
            pe.wait_ge(wr_ready, 1)
            for t in range(T):
                for k in range(KB):
                    hi, lo = (m[:, k, t * P:(t + 1) * P] for m in (xt_hi, xt_lo))
                    last = split_product(psum[0][:, t * EXPERTS:(t + 1) * EXPERTS], hi, lo,
                                         wr_hi[:, k, :], wr_lo[:, k, :], k == 0, k == KB - 1)
            last.then_inc(logits_done, 1)
            pe.wait_ge(mask_ready, 1)
            masks = route[:, 8, :, :]
            precedes, ones = table[:, C_PRECEDES:C_PRECEDES + P], table[:, C_ONES:C_ONES + P]
            pe.matmul(psum[1][:, 0:EXPERTS], precedes, masks[:, 0, :], start=True, stop=True)
            pe.matmul(psum[1][:, EXPERTS:2 * EXPERTS], ones, masks[:, 0, :], start=True, stop=False)
            pe.matmul(psum[1][:, EXPERTS:2 * EXPERTS], precedes, masks[:, 1, :], start=False, stop=True)
            for t in range(T):
                last = pe.matmul(psum[1][:, 2 * EXPERTS:3 * EXPERTS], ones, masks[:, t, :], start=(t == 0), stop=(t == 1))
            last.then_inc(places_done, 1)

            def gather(k):
                pe.wait_ge(pick_ready, plus(k, 1))
                for banks, tok in (((2, 3), tok_hi), ((6, 7), tok_lo)):
                    for b in range(KB):
                        for t in range(T):
                            last = pe.matmul(psum[banks[b // 4]][:, (b % 4) * P:(b % 4 + 1) * P],
                                             tok[:, t, b * P:(b + 1) * P], pick[:, t, :],
                                             start=(t == 0), stop=(t == T - 1))
                last.then_inc(gathered, 1)

            def scatter(k):
                pe.wait_ge(y_lo_ready, plus(k, 1))
                for t in range(T):
                    for h in range(2):
                        bank = psum[(2, 3, 6, 7)[2 * t + h]]
                        c = slice(h * COLS, (h + 1) * COLS)
                        pe.matmul(bank[:], pickT[:, t * P:(t + 1) * P], y_hi[:, c], start=True, stop=False)
                        pe.matmul(bank[:], pickT[:, t * P:(t + 1) * P], y_lo[:, c],
                                  start=False, stop=True).then_inc(scattered, 1)

            pe.wait_ge(tok_lo_ready, 1)
            gather(0)
            with pe.Fori(0, ITEMS) as k:
                runs = pe.value_load(plan[0:1, 0, bass.ds(k + 1, 1)], min_val=0, max_val=1)
                with pe.If(runs > 0):
                    def scatter_and_turn():
                        scatter(k)
                        pe.wait_ge(g_ready, k * STEPS + (FFN_EVENTS + 1))
                        for t in range(T):
                            last = pe.transpose(psum[0][:, t * P:(t + 1) * P], pick[:, t, :].bitcast(F32), ident)
                        last.then_inc(pick_turned, 1)

                    def gather_next():
                        pe.wait_ge(added, k * 4 + 4)
                        gather(k + 1)

                    pe.wait_ge(slot_lo_ready, k + 1)
                    swiglu(MOE, k * PIECES_PER_SWIGLU, k * STEPS + FFN_EVENTS, slot_hi, slot_lo, 1, [[4, 5]],
                           after_first=scatter_and_turn, before_last=gather_next,
                           after_turn=lambda: pe.wait_ge(pickT_ready, k + 1))
            runs_n = pe.value_load(plan[0:1, 1, 0:1], min_val=1, max_val=ITEMS - 1)
            scatter(runs_n)

        @block.scalar
        def _(act):
            done = [0]

            def hi_part(n, base, landings):
                act.wait_ge(landed[n % RAW_SLOTS], plus(landings, 16 * (n // RAW_SLOTS + 1)))
                if not isinstance(base, int) or n >= SPLIT_SLOTS:
                    act.wait_ge(piece_used, plus(base, n + 1 - SPLIT_SLOTS))
                act.activation(w_hi[:, n % SPLIT_SLOTS, :], raw[:, n % RAW_SLOTS, :], ACT.Copy).then_inc(hi_ready, 1)

            def split_to(n):
                while done[0] < n:
                    hi_part(done[0], 0, 0)
                    done[0] += 1

            def turned_hi(group, blk, banks=None):
                act.wait_ge(turned, group + 1)
                act.activation(xt_hi[:, blk:blk + 2, :], psum[TURN_BANKS[group]][:].rearrange("p (k s) -> p k s", k=2),
                               ACT.Copy).then_inc(xt_hi_ready, 1)

            def read_linear(last_piece, banks, dst, fn=ACT.Copy):
                split_to(last_piece + 2)
                act.wait_ge(piece_used, last_piece + 1)
                for t in range(T):
                    last = act.activation(dst[t], psum[banks[t]][:], fn)
                last.then_inc(lin_read, 1)

            def root(number, dst, src):
                act.wait_ge(var_ready, number)
                act.activation(dst, src, ACT.Sqrt).then_inc(std_ready, 1)

            def nothing():
                pass

            def swiglu(n, base, landings, events, tiles, split_before, after_first=nothing):
                h1 = [2, 3] if tiles == 2 else [1]

                def silu_step(n, base, now):
                    act.wait_ge(piece_used, plus(base, n + 1))
                    for t in range(tiles):
                        act.activation(silu[:, t, :], psum[h1[t]][:], ACT.Silu).then_inc(silu_ready, 1)

                def turned_g(now):
                    for t in range(tiles):
                        act.wait_ge(g_turned, plus(now, t + 1))
                        act.activation(gT_hi[:, :, t * P:(t + 1) * P], psum[h1[t]][:].rearrange("p (b s) -> p b s", b=FB),
                                       ACT.Copy).then_inc(gT_hi_ready, 1)

                for i in range(split_before, 6):
                    hi_part(n + i, base, landings)
                silu_step(n + 3, base, events)
                after_first()
                turned_g(events)
                with act.Fori(1, STEPS) as j:
                    here = base + (j - 1) * 6
                    land = landings + (j - 1) * 16
                    now = events + j * tiles
                    for i in range(2, 6):
                        hi_part(n + 4 + i, here, land)
                    silu_step(n + 7, here, now)
                    for i in range(6, 8):
                        hi_part(n + 4 + i, here, land)
                    turned_g(now)

            split_to(1)
            for i in range(4):
                turned_hi(TURN_X + i, 2 * i)
            act.wait_ge(lam_dotted, 1)
            act.activation(lam_exp, lam_dot, ACT.Exp).then_inc(lam_exped, 1)

            read_linear(EVEN_IN + 1, [0, 1], [q_nat[:, t, :] for t in range(T)])
            read_linear(EVEN_IN + 3, [2, 3], [k_nat[:, t, :] for t in range(T)])
            read_linear(EVEN_IN + 5, [0, 1], [va[:, t, :] for t in range(T)])
            act.wait_ge(qk_turned, 1)
            for i in range(2):
                last = act.activation(qT[:, 2 * i:2 * i + 2, :], psum[4 + i][:].rearrange("p (h s) -> p h s", h=2), ACT.Copy)
            last.then_inc(qT_ready, 1)
            read_linear(EVEN_IN + 7, [2, 3], [v_act[:, t, :] for t in range(T)], ACT.Gelu)

            def exps(h):
                act.wait_ge(top_ready, h + 1)
                b = h % 2
                for c in range(2):
                    for t, (c0, c1) in enumerate(((0, P), (P, SCORE_COLS))):
                        i = 2 * c + t
                        last = act.activation(prob[:, b, c, c0:c1], prob[:, b, c, c0:c1], ACT.Exp,
                                              bias=neg_top[:, b, i:i + 1], accum_out=total[:, b, i:i + 1])
                last.then_inc(exp_ready, 1)

            def turned_attn(h):
                act.wait_ge(attn_turned, h + 1)
                if h >= 2:
                    act.wait_ge(pv_done, h - 1)
                act.activation(attnT[:, h % 2, :], psum[2 + h % 2][:, 0:SCORE_COLS], ACT.Copy).then_inc(attnT_ready, 1)

            read_linear(EVEN_IN + 9, [0, 1], [u_act[:, t, :] for t in range(T)], ACT.Gelu)
            root(1, std, var_eps)
            exps(0)
            exps(1)
            turned_attn(0)
            exps(2)
            turned_attn(1)
            exps(3)
            turned_attn(2)
            turned_attn(3)
            for i in range(2):
                turned_hi(TURN_MIX + i, 2 * i)
            root(2, sub_std, sub_ss)
            for i in range(2, 4):
                turned_hi(TURN_MIX + i, 2 * i)
            split_to(EVEN_OUT + 6)
            root(3, std[:, 0:T], var_eps[:, 0:T])
            for i in range(4):
                turned_hi(TURN_X1 + i, 2 * i)

            swiglu(FFN, 0, 0, 0, T, done[0] - FFN)
            done[0] = ODD_IN
            split_to(ODD_IN + 2)
            root(4, std[:, 0:T], var_eps[:, 0:T])
            for i in range(4):
                turned_hi(TURN_X2 + i, 2 * i)

            for c in range(ODD_CHUNKS):
                banks = [[0, 1], [2, 3]][c % 2]
                if c < 4:
                    if c >= 2:
                        act.wait_ge(ret_turned, c - 1)
                    dst, fn = [qk_nat[:, c % 2, t, :] for t in range(T)], ACT.Copy
                elif c < 8:
                    dst, fn = [r_v[:, t, (c - 4) * COLS:(c - 3) * COLS] for t in range(T)], ACT.Copy
                else:
                    dst, fn = [r_g[:, t, (c - 8) * COLS:(c - 7) * COLS] for t in range(T)], ACT.Silu
                if c >= 10:
                    root(4 + c - 9, ret_std[:, 0:T], ret_var[:, 0:T])
                    split_to(ODD_IN + 2 * c + 2)
                    for i in range(2):
                        turned_hi(TURN_O + 2 * (c - 10) + i, o_block(4 * (c - 10) + 2 * i))
                read_linear(ODD_IN + 2 * c + 1, banks, dst, fn)
            for h in (2, 3):
                root(5 + h, ret_std[:, 0:T], ret_var[:, 0:T])
                split_to(ODD_OUT + (2 if h == 2 else 8))
                for i in range(2):
                    turned_hi(TURN_O + 2 * h + i, o_block(4 * h + 2 * i))
            root(9, std[:, 0:T], var_eps[:, 0:T])

            for t in range(T):
                act.wait_ge(x_ready, 3 * T)
                last = act.activation(tok_hi[:, t, :], x[:, t, :], ACT.Copy)
            last.then_inc(tok_hi_ready, 1)
            act.wait_ge(router_landed, 32)
            act.activation(wr_hi[:], wr[:], ACT.Copy).then_inc(wr_hi_ready, 1)
            for i in range(4):
                turned_hi(TURN_X3 + i, 2 * i)
            act.wait_ge(gap_ready, 1)
            act.activation(odds, gap, ACT.Exp).then_inc(odds_ready, 1)

            def slots_hi(k):
                act.wait_ge(gathered, plus(k, 1))
                for i in range(2):
                    last = act.activation(slot_hi[:, 4 * i:4 * i + 4, :],
                                          psum[2 + i][:].rearrange("p (k s) -> p k s", k=4), ACT.Copy)
                last.then_inc(slot_hi_ready, 1)

            def rows_hi(k):
                for h in range(2):
                    act.activation(y_hi[:, h * COLS:(h + 1) * COLS], psum[4 + h][:], ACT.Copy).then_inc(y_hi_ready, 1)

            split_to(MOE + 2)
            slots_hi(0)
            with act.Fori(0, ITEMS) as k:
                runs = act.value_load(plan[0:1, 0, bass.ds(k + 1, 1)], min_val=0, max_val=1)
                more = act.value_load(plan[0:1, 0, bass.ds(k + 2, 1)], min_val=0, max_val=1)
                with act.If(runs > 0):
                    pieces = k * PIECES_PER_SWIGLU

                    def turned_pick():
                        act.wait_ge(pick_turned, k + 1)
                        act.activation(pickT[:], psum[0][:, 0:SEQ], ACT.Copy).then_inc(pickT_ready, 1)

                    act.wait_ge(piece_used, pieces + MOE)
                    rows_hi(k)
                    swiglu(MOE, pieces, k * (16 * STEPS), k * STEPS + FFN_EVENTS, 1, 2, after_first=turned_pick)
                    slots_hi(k + 1)
                    with act.If(more > 0):
                        for i in range(2):
                            hi_part(MOE + PIECES_PER_SWIGLU + i, pieces, k * (16 * STEPS))
            runs_n = act.value_load(plan[0:1, 1, 0:1], min_val=1, max_val=ITEMS - 1)
            act.wait_ge(piece_used, runs_n * PIECES_PER_SWIGLU + MOE)
            rows_hi(runs_n)
            root(10, std[:, 0:T], var_eps[:, 0:T])

        @block.vector
        def _(dve):
            own = Chain(dve, vector_step)
            done = [0]

            def lo_part(n, base):
                dve.wait_ge(hi_ready, plus(base, n + 1))
                dve.tensor_tensor(w_lo[:, n % SPLIT_SLOTS, :], raw[:, n % RAW_SLOTS, :],
                                  w_hi[:, n % SPLIT_SLOTS, :].bitcast(F32), ALU.subtract).then_inc(lo_ready, 1)

            def split_to(n):
                while done[0] < n:
                    lo_part(done[0], 0)
                    done[0] += 1

            def turned_lo(group, blk):
                dve.wait_ge(xt_hi_ready, group + 1)
                dve.tensor_tensor(xt_lo[:, blk:blk + 2, :], psum[TURN_BANKS[group]][:].rearrange("p (k s) -> p k s", k=2),
                                  xt_hi[:, blk:blk + 2, :].bitcast(F32), ALU.subtract).then_inc(xt_lo_ready, 1)

            def inverse_root(number, dst, src, from_act):
                own.link(dve.tensor_scalar(src, src, EPS, None, ALU.add))
                dve.sem_inc(var_ready, 1)
                dve.wait_ge(std_ready, number)
                own.link(dve.reciprocal(dst, from_act))

            def layer_norm(number, root_no, last_piece, banks):
                if banks:
                    split_to(last_piece + 1)
                    dve.wait_ge(piece_used, last_piece + 1)
                for t in range(T):
                    for h in range(2):
                        part = x[:, t, h * COLS:(h + 1) * COLS]
                        if banks:
                            ins = dve.scalar_tensor_tensor(out=part, in0=part, scalar=ALPHA, in1=psum[banks[t][h]][:],
                                                           op0=ALU.mult, op1=ALU.add)
                            if (t, h) == (1, 1):
                                own.link(ins)
                for t in range(T):
                    for h in range(2):
                        ins = dve.bn_stats(stats[:, 2 * t + h, :], x[:, t, h * COLS:(h + 1) * COLS])
                own.link(ins)
                for t in range(T):
                    ins = dve.bn_aggr(mean_var[:, t, :], stats[:, 2 * t:2 * t + 2, :])
                own.link(ins)
                own.link(dve.tensor_copy(var_eps[:, 0:T], mean_var[:, 0:T, 1]))
                inverse_root(root_no, rstd[:, 0:T], var_eps[:, 0:T], std[:, 0:T])
                dve.wait_ge(vec_landed[(0, 1, 3, 4)[number]], 32)
                for t in range(T):
                    own.link(dve.tensor_scalar(x[:, t, :], x[:, t, :], mean_var[:, t, 0:1], rstd[:, t:t + 1],
                                               ALU.subtract, ALU.mult))
                    own.link(dve.tensor_tensor(x[:, t, :], x[:, t, :], vec[:, 0:D], ALU.mult))
                    dve.tensor_tensor(x[:, t, :], x[:, t, :], vec[:, D:2 * D], ALU.add).then_inc(x_ready, 1)

            def nothing():
                pass

            def swiglu(n, base, events, tiles, split_before, after_first=nothing):
                h3, h1 = [0, 1][:tiles], [2, 3] if tiles == 2 else [1]

                def product(now):
                    for t in range(tiles):
                        dve.wait_ge(silu_ready, plus(now, t + 1))
                        dve.tensor_tensor(g[:, t, :], silu[:, t, :], psum[h3[t]][:], ALU.mult).then_inc(g_ready, 1)

                def turned_g(now):
                    for t in range(tiles):
                        dve.wait_ge(gT_hi_ready, plus(now, t + 1))
                        dve.tensor_tensor(gT_lo[:, :, t * P:(t + 1) * P], psum[h1[t]][:].rearrange("p (b s) -> p b s", b=FB),
                                          gT_hi[:, :, t * P:(t + 1) * P].bitcast(F32), ALU.subtract).then_inc(gT_lo_ready, 1)

                for i in range(split_before, 6):
                    lo_part(n + i, base)
                product(events)
                turned_g(events)
                after_first()
                with dve.Fori(1, STEPS) as j:
                    here = base + (j - 1) * 6
                    now = events + j * tiles
                    for i in range(2, 6):
                        lo_part(n + 4 + i, here)
                    product(now)
                    for i in range(6, 8):
                        lo_part(n + 4 + i, here)
                    turned_g(now)

            split_to(1)
            for i in range(4):
                turned_lo(TURN_X + i, 2 * i)

            dve.wait_ge(gating_landed, 16 * 9)
            dve.wait_ge(table_landed, 16)
            for i in range(2):
                ins = dve.tensor_tensor_reduce(prob[:, 0, i, 0:DH], lam_in[:, 2 * i, :], lam_in[:, 2 * i + 1, :], 1.0, 0.0,
                                               ALU.mult, ALU.add, lam_dot[:, i:i + 1])
            own.link(ins)
            dve.sem_inc(lam_dotted, 1)
            for gr in range(GROUPS):
                ins = dve.tensor_tensor(gate_w[:, gr, :], gate_w[:, gr, :], table[:, C_CAUSAL:C_CAUSAL + P], ALU.mult)
            own.link(ins)
            own.link(dve.tensor_scalar(sub_gain[:], sub_gain[:], 1.0 - LAM_INIT, None, ALU.mult))
            split_to(EVEN_IN + 4)
            dve.wait_ge(lam_exped, 1)
            own.link(dve.tensor_tensor(neg_lam, lam_exp[:, 1:2], lam_exp[:, 0:1], ALU.subtract))
            own.link(dve.tensor_scalar(neg_lam, neg_lam, -LAM_INIT, None, ALU.add))
            split_to(EVEN_IN + 6)
            dve.wait_ge(qk_turned, 2)
            for i in range(2):
                ins = dve.tensor_copy(kT[:, 2 * i:2 * i + 2, :], psum[6 + i][:].rearrange("p (h s) -> p h s", h=2))
            ins.then_inc(kT_ready, 1)
            split_to(EVEN_IN + 9)

            def softmax_top(h):
                b = h % 2
                dve.wait_ge(scores_done, h + 1)
                for c in range(2):
                    ins = dve.scalar_tensor_tensor(out=prob[:, b, c, :], in0=psum[4 + 2 * b + c][:, 0:SCORE_COLS],
                                                   scalar=DH ** -0.5, in1=bias[:, h, :], op0=ALU.mult, op1=ALU.add)
                own.link(ins)
                dve.sem_inc(scores_read, 1)
                if h == HEADS - 1:
                    dve.sem_inc(bias_used, 1)
                for c in range(2):
                    for t, (c0, c1) in enumerate(((0, P), (P, SCORE_COLS))):
                        ins = dve.reduce_max(top[:, b, 2 * c + t:2 * c + t + 1], prob[:, b, c, c0:c1], AX_X)
                own.link(ins)
                dve.tensor_scalar(neg_top[:, b, :], top[:, b, :], -1.0, None, ALU.mult).then_inc(top_ready, 1)

            def softmax_combine(h):
                b = h % 2
                dve.wait_ge(exp_ready, h + 1)
                own.link(dve.reciprocal(scale[:, b, :], total[:, b, :]))
                own.link(dve.tensor_scalar(scale[:, b, 2:4], scale[:, b, 2:4], neg_lam, None, ALU.mult))
                for t, (c0, c1) in enumerate(((0, P), (P, SCORE_COLS))):
                    ins = dve.tensor_scalar(prob[:, b, 1, c0:c1], prob[:, b, 1, c0:c1], scale[:, b, 2 + t:3 + t],
                                            None, ALU.mult)
                own.link(ins)
                if h >= 2:
                    dve.wait_ge(attn_turned, h - 1)
                for t, (c0, c1) in enumerate(((0, P), (P, SCORE_COLS))):
                    ins = dve.scalar_tensor_tensor(out=attn[:, b, c0:c1], in0=prob[:, b, 0, c0:c1],
                                                   scalar=scale[:, b, t:t + 1], in1=prob[:, b, 1, c0:c1],
                                                   op0=ALU.mult, op1=ALU.add)
                own.link(ins)
                dve.sem_inc(attn_ready, 1)

            dve.wait_ge(bias_landed, 16)
            dve.wait_ge(lin_read, 4)
            for t in range(T):
                for gr in range(GROUPS):
                    ins = dve.bn_stats(stats[:, 4 * t + gr, :], v_act[:, t, gr * P:(gr + 1) * P])
            own.link(ins)
            for i in range(8):
                ins = dve.bn_aggr(mean_var[:, i, :], stats[:, i:i + 1, :])
            own.link(ins)
            own.link(dve.tensor_copy(var_eps, mean_var[:, :, 1]))
            own.link(dve.tensor_scalar(var_eps, var_eps, EPS, None, ALU.add))
            dve.sem_inc(var_ready, 1)
            split_to(EVEN_IN + 10)
            softmax_top(0)
            softmax_top(1)
            dve.wait_ge(std_ready, 1)
            own.link(dve.reciprocal(rstd, std))
            for t in range(T):
                for gr in range(GROUPS):
                    i = 4 * t + gr
                    part = v_act[:, t, gr * P:(gr + 1) * P]
                    ins = dve.tensor_scalar(part, part, mean_var[:, i, 0:1], rstd[:, i:i + 1], ALU.subtract, ALU.mult)
                own.link(ins)
                own.link(dve.tensor_tensor(v_act[:, t, :], v_act[:, t, :], v_gain[:], ALU.mult))
                own.link(dve.tensor_tensor(v_act[:, t, :], v_act[:, t, :], v_bias[:], ALU.add))
            dve.sem_inc(v_ready, 1)
            softmax_combine(0)
            softmax_top(2)
            softmax_combine(1)
            softmax_top(3)
            dve.wait_ge(gating_done, 1)
            dve.wait_ge(lin_read, 5)
            for t in range(T):
                for gr in range(GROUPS):
                    c = slice(gr * P, (gr + 1) * P)
                    ins = dve.scalar_tensor_tensor(out=mix[:, t, c], in0=psum[4 + t][:, c], scalar=b_s[:, gr:gr + 1],
                                                   in1=u_act[:, t, c], op0=ALU.add, op1=ALU.mult)
            own.link(ins)
            dve.sem_inc(mix_ready, 1)
            softmax_combine(2)
            softmax_combine(3)
            for i in range(2):
                turned_lo(TURN_MIX + i, 2 * i)
            dve.wait_ge(pv_done, HEADS)
            for t in range(T):
                ins = dve.tensor_copy(va[:, t, :], psum[t][:])
            own.link(ins)
            for t in range(T):
                ins = dve.tensor_tensor(q_nat[:, t, :], va[:, t, :], va[:, t, :], ALU.mult)
            own.link(ins)
            own.link(dve.tensor_reduce(sub_ss, q_nat[:].rearrange("p t (h d) -> p (t h) d", h=HEADS), AX_X, ALU.add))
            own.link(dve.tensor_scalar(sub_ss, sub_ss, 1.0 / P, EPS, ALU.mult, ALU.add))
            dve.sem_inc(var_ready, 1)
            dve.wait_ge(std_ready, 2)
            own.link(dve.reciprocal(sub_ss, sub_std))
            for t in range(T):
                for h in range(HEADS):
                    c = slice(h * P, (h + 1) * P)
                    ins = dve.scalar_tensor_tensor(out=mix[:, t, 512 + h * P:512 + (h + 1) * P], in0=va[:, t, c],
                                                   scalar=sub_ss[:, 4 * t + h:4 * t + h + 1], in1=sub_gain[:],
                                                   op0=ALU.mult, op1=ALU.mult)
            own.link(ins)
            dve.sem_inc(mix_ready, 1)
            for i in range(2, 4):
                turned_lo(TURN_MIX + i, 2 * i)
            split_to(EVEN_OUT + 4)
            layer_norm(0, 3, EVEN_OUT + 3, [[0, 1], [4, 5]])
            split_to(EVEN_OUT + 6)
            for i in range(4):
                turned_lo(TURN_X1 + i, 2 * i)

            swiglu(FFN, 0, 0, T, done[0] - FFN)
            done[0] = ODD_IN
            layer_norm(1, 4, ODD_IN - 1, [[4, 5], [6, 7]])
            split_to(ODD_IN + 2)
            for i in range(4):
                turned_lo(TURN_X2 + i, 2 * i)

            def turned_qk(c):
                dve.wait_ge(ret_turned, c + 1)
                dst = (r_qT, r_kT)[c // 2]
                for i in range(2):
                    b = 4 * (c % 2) + 2 * i
                    ins = dve.tensor_copy(dst[:, b:b + 2, :], psum[4 + 2 * (c % 2) + i][:].rearrange("p (k s) -> p k s", k=2))
                ins.then_inc(ret_T_ready, 1)

            def decay(h):
                dve.wait_ge(ret_scores, h + 1)
                dve.tensor_tensor(decayed[:, h % 2, :], psum[4][:, 0:SCORE_COLS], bias[:, h, :],
                                  ALU.mult).then_inc(ret_decayed, 1)

            def head_norm(h):
                dve.wait_ge(ret_out, h + 1)
                for t in range(T):
                    ins = dve.bn_stats(stats[:, t, :], psum[5 + t][:])
                own.link(ins)
                for t in range(T):
                    ins = dve.bn_aggr(ret_mv[:, t, :], stats[:, t:t + 1, :])
                own.link(ins)
                own.link(dve.tensor_copy(ret_var[:, 0:T], ret_mv[:, 0:T, 1]))
                inverse_root(5 + h, ret_rstd[:, 0:T], ret_var[:, 0:T], ret_std[:, 0:T])
                dve.wait_ge(vec_landed[2], 16)
                dve.wait_ge(lin_read, 5 + 9 + h)
                for t in range(T):
                    own.link(dve.tensor_scalar(o_norm[:], psum[5 + t][:], ret_mv[:, t, 0:1], ret_rstd[:, t:t + 1],
                                               ALU.subtract, ALU.mult))
                    own.link(dve.tensor_tensor(o_norm[:], o_norm[:], vec[:, h * RET_V:(h + 1) * RET_V], ALU.mult))
                    part = r_g[:, t, h * RET_V:(h + 1) * RET_V]
                    own.link(dve.tensor_tensor(part, o_norm[:], part, ALU.mult))
                dve.sem_inc(o_ready, 1)
    
            for c in range(ODD_CHUNKS):
                split_to(ODD_IN + 2 * c + 3)
                if 1 <= c <= 4:
                    turned_qk(c - 1)
                if c == 8:
                    dve.wait_ge(decay_landed, 16)
                if c >= 9:
                    head_norm(c - 9)
                    split_to(ODD_IN + 2 * c + 4)
                    for i in range(2):
                        turned_lo(TURN_O + 2 * (c - 9) + i, o_block(4 * (c - 9) + 2 * i))
                if c >= 8:
                    decay(c - 8)
            split_to(ODD_OUT + 2)
            head_norm(3)
            split_to(ODD_OUT + 8)
            for i in range(2):
                turned_lo(TURN_O + 6 + i, o_block(12 + 2 * i))
            layer_norm(2, 9, ODD_OUT + 7, [[0, 1], [4, 7]])

            dve.wait_ge(tok_hi_ready, 1)
            for t in range(T):
                ins = dve.tensor_tensor(tok_lo[:, t, :], x[:, t, :], tok_hi[:, t, :].bitcast(F32), ALU.subtract)
            ins.then_inc(tok_lo_ready, 1)
            dve.wait_ge(wr_hi_ready, 1)
            dve.tensor_tensor(wr_lo[:], wr[:], wr_hi[:].bitcast(F32), ALU.subtract).then_inc(wr_ready, 1)
            for i in range(4):
                turned_lo(TURN_X3 + i, 2 * i)
            for t in range(T):
                ins = dve.tensor_scalar(x[:, t, :], x[:, t, :], ALPHA, None, ALU.mult)
            own.link(ins)
            logits, is_top, rank, first, rest, is_next, second, gates, mask, spare_r = (route[:, i, :, :] for i in range(10))
            rev = table[:, C_REV:C_REV + EXPERTS]
            dve.wait_ge(logits_done, 1)
            dve.wait_ge(router_landed, 32)
            for t in range(T):
                ins = dve.tensor_tensor(logits[:, t, :], psum[0][:, t * EXPERTS:(t + 1) * EXPERTS], rb[:], ALU.add)
            own.link(ins)

            def pick_first(values, peak, equal, chosen):
                own.link(dve.reduce_max(peak, values, AX_X))
                for t in range(T):
                    ins = dve.scalar_tensor_tensor(out=equal[:, t, :], in0=values[:, t, :], scalar=peak[:, t:t + 1],
                                                   in1=rev, op0=ALU.is_equal, op1=ALU.mult)
                own.link(ins)
                own.link(dve.reduce_max(best, equal, AX_X))
                for t in range(T):
                    ins = dve.tensor_scalar(chosen[:, t, :], equal[:, t, :], best[:, t:t + 1], None, ALU.is_equal)
                own.link(ins)

            pick_first(logits, peak1, is_top, first)
            own.link(dve.scalar_tensor_tensor(out=rest, in0=first, scalar=LOWEST, in1=logits, op0=ALU.mult, op1=ALU.add))
            pick_first(rest, peak2, is_next, second)
            own.link(dve.tensor_tensor(mask, first, second, ALU.add))
            dve.sem_inc(mask_ready, 1)
            own.link(dve.tensor_tensor(gap, peak2, peak1, ALU.subtract))
            dve.sem_inc(gap_ready, 1)
            dve.wait_ge(odds_ready, 1)
            own.link(dve.tensor_scalar(share1, odds, 1.0, None, ALU.add))
            own.link(dve.reciprocal(share1, share1))
            own.link(dve.tensor_tensor(share2, odds, share1, ALU.mult))
            for t in range(T):
                ins = dve.tensor_scalar(spare_r[:, t, :], second[:, t, :], share2[:, t:t + 1], None, ALU.mult)
            own.link(ins)
            for t in range(T):
                ins = dve.scalar_tensor_tensor(out=gates[:, t, :], in0=first[:, t, :], scalar=share1[:, t:t + 1],
                                               in1=spare_r[:, t, :], op0=ALU.mult, op1=ALU.add)
            own.link(ins)
            dve.wait_ge(places_done, 1)
            own.link(dve.tensor_scalar(spare_r, mask, -NOT_CHOSEN, NOT_CHOSEN, ALU.mult, ALU.add))
            places = psum[1][:, 0:T * EXPERTS].rearrange("p (t e) -> p t e", t=T)
            own.link(dve.tensor_tensor(slot_no[:, :, 0:EXPERTS], spare_r, places, ALU.add))
            dve.tensor_scalar(slot_no[:, :, EXPERTS:ITEMS], slot_no[:, :, 0:EXPERTS], float(-P), None, ALU.add)
            for i in range(TILES):
                dve.tensor_copy(gate[:, :, i * EXPERTS:(i + 1) * EXPERTS], gates)
            own.link(dve.memset(plan_f[:], 0.0))
            for i in range(TILES):
                ins = dve.tensor_scalar(plan_f[:, 0, 16 + i * EXPERTS:16 + (i + 1) * EXPERTS],
                                        psum[1][:, 2 * EXPERTS:3 * EXPERTS], float(i * P), None, ALU.is_gt)
            own.link(ins)
            for i in range(4):
                own.link(dve.tensor_tensor(plan_f[:, i + 1, 16:32], plan_f[:, i, 16:32],
                                           plan_f[:, i, 16 - 2 ** i:32 - 2 ** i], ALU.add))
            own.link(dve.tensor_tensor(plan_f[:, 5, 16:32], plan_f[:, 4, 16:32], plan_f[:, 0, 16:32], ALU.subtract))
            numbers = table[:, C_ITEM:C_ITEM + ITEMS]
            for k in range(ITEMS):
                ins = dve.scalar_tensor_tensor(out=order[:, k, :], in0=plan_f[:, 5, 16:32], scalar=float(k),
                                               in1=plan_f[:, 0, 16:32], op0=ALU.is_equal, op1=ALU.mult)
            own.link(ins)
            own.link(dve.memset(plan_g[:], 0.0))
            own.link(dve.tensor_reduce(plan_g[:, 0, 1:ITEMS + 1], order[:], AX_X, ALU.add))
            for k in range(ITEMS):
                ins = dve.tensor_tensor(order[:, k, :], order[:, k, :], numbers, ALU.mult)
            own.link(ins)
            own.link(dve.tensor_reduce(plan_g[:, 1, 1:ITEMS + 1], order[:], AX_X, ALU.add))
            own.link(dve.tensor_scalar(plan_g[:, 2, :], plan_g[:, 1, :], EXPERTS - 0.5, -float(EXPERTS), ALU.is_gt, ALU.mult))
            own.link(dve.tensor_tensor(plan_g[:, 2, :], plan_g[:, 2, :], plan_g[:, 1, :], ALU.add))
            own.link(dve.tensor_copy(plan_g[:, 1, 0:1], plan_f[:, 4, 31:32]))
            own.link(dve.tensor_copy(plan[:], plan_g[:]))
            own.link(dve.memset(pickT[:].bitcast(F32), 0.0))
            dve.sem_inc(plan_ready, 1)

            def slots_lo(k):
                dve.wait_ge(slot_hi_ready, plus(k, 1))
                for i in range(2):
                    ins = dve.tensor_copy(slot_lo[:, 4 * i:4 * i + 4, :],
                                          psum[6 + i][:].rearrange("p (k s) -> p k s", k=4))
                ins.then_inc(slot_lo_ready, 1)

            def rows_lo(k):
                for h in range(2):
                    c = slice(h * COLS, (h + 1) * COLS)
                    dve.wait_ge(y_hi_ready, k * 2 + (h + 1))
                    ins = dve.tensor_tensor(y_lo[:, c], psum[4 + h][:], y_hi[:, c].bitcast(F32), ALU.subtract)
                ins.then_inc(y_lo_ready, 1)

            def add_rows(k, item):
                for t in range(T):
                    for h in range(2):
                        part = x[:, t, h * COLS:(h + 1) * COLS]
                        dve.wait_ge(scattered, k * 4 + (2 * t + h + 1))
                        dve.scalar_tensor_tensor(out=part, in0=psum[(2, 3, 6, 7)[2 * t + h]][:],
                                                 scalar=gate[:, t, bass.ds(item, 1)], in1=part,
                                                 op0=ALU.mult, op1=ALU.add).then_inc(added, 1)

            split_to(MOE + 2)
            slots_lo(0)
            with dve.Fori(0, ITEMS) as k:
                runs = dve.value_load(plan[0:1, 0, bass.ds(k + 1, 1)], min_val=0, max_val=1)
                more = dve.value_load(plan[0:1, 0, bass.ds(k + 2, 1)], min_val=0, max_val=1)
                with dve.If(runs > 0):
                    last_item = dve.value_load(plan[0:1, 1, bass.ds(k, 1)], min_val=0, max_val=ITEMS - 1)
                    pieces = k * PIECES_PER_SWIGLU
                    rows_lo(k)
                    swiglu(MOE, pieces, k * STEPS + FFN_EVENTS, 1, 2, after_first=lambda: add_rows(k, last_item))
                    slots_lo(k + 1)
                    with dve.If(more > 0):
                        for i in range(2):
                            lo_part(MOE + PIECES_PER_SWIGLU + i, pieces)
            runs_n = dve.value_load(plan[0:1, 1, 0:1], min_val=1, max_val=ITEMS - 1)
            rows_lo(runs_n)
            last_item = dve.value_load(plan[0:1, 1, bass.ds(runs_n, 1)], min_val=0, max_val=ITEMS - 1)
            add_rows(runs_n, last_item)
            dve.wait_ge(added, runs_n * 4 + 4)
            own.link(dve.memset(stats[:], 0.0))
            layer_norm(3, 10, None, None)


def kernel(**inputs):
    import numpy as _np
    import concourse.bacc as _bacc
    from concourse import mybir as _mybir
    from concourse.bass_utils import run_bass_kernel_spmd as _run

    def layer(name):
        return _np.asarray(inputs[name])[0]

    table, alibi, decay = constants()
    arrays = {"x": _np.asarray(inputs["x"])[0], "table": table, "alibi": alibi, "decay": decay}
    for name in ("even_w_in", "even_w_o", "ffn_w1", "ffn_w3", "ffn_w2", "odd_w_in", "odd_w_o", "router_w",
                 "moe_w1", "moe_w3", "moe_w2"):
        arrays[name] = layer(name)
    for name in ("even_v_ln_g", "even_v_ln_b", "even_lam_q1", "even_lam_k1", "even_lam_q2", "even_lam_k2",
                 "even_subln_g", "even_ln1_g", "even_ln1_b", "even_ln2_g", "even_ln2_b", "odd_gn_g",
                 "odd_ln1_g", "odd_ln1_b", "router_b", "odd_ln2_g", "odd_ln2_b"):
        arrays[name] = layer(name).reshape(-1)
    arrays["even_w_s_t"] = layer("even_w_s").transpose(2, 0, 1)
    arrays["even_b_s_t"] = layer("even_b_s").T

    nc = _bacc.Bacc("TRN2", target_bir_lowering=False, num_devices=1)
    aps, feed = {}, {}
    for name, value in arrays.items():
        value = _np.ascontiguousarray(value)
        feed[f"in_{name}"] = value
        aps[name] = nc.dram_tensor(f"in_{name}", value.shape, _mybir.dt.from_np(value.dtype), kind="ExternalInput").ap()
    out = nc.dram_tensor("out_x", (SEQ, D), F32, kind="ExternalOutput").ap()
    hybrid_trunk(nc, aps, out)
    r = _run(nc, [feed], core_ids=[0])
    return r.results[0]["out_x"].reshape(1, SEQ, D)
```

```python
import math
from contextlib import ExitStack

import numpy as np

import concourse.bass as bass
from concourse import mybir

F32 = mybir.dt.float32
F32R = mybir.dt.float32r
I32 = mybir.dt.int32
ALU = mybir.AluOpType
ACT = mybir.ActivationFunctionType
AX_X = mybir.AxisListType.X

P = 128
SEQ = 256
T = SEQ // P
D = 1024
KB = D // P
DEPTH = 2
ALPHA = (2.0 * DEPTH) ** 0.25
EPS = 1e-5
COLS = 512
PIECE = 2048
FF = 7 * D // 2
STEPS = FF // COLS
FB = COLS // P

GROUPS = 4
HEADS = 4
DH = 64
LAM_INIT = 0.8 - 0.6 * math.exp(0.0)
RET_HEADS = 4
RET_V = 512
EXPERTS = 8
TILES = 2
ITEMS = TILES * EXPERTS
TURNS = EXPERTS + 2 * SEQ // (P + 1)
NOT_CHOSEN = 1000.0
LOWEST = -3.0e38

RAW_SLOTS = 6
SPLIT_SLOTS = 3
PIECES_PER_SWIGLU = 6 * STEPS

EVEN_IN = 0
EVEN_OUT = EVEN_IN + 10
FFN = EVEN_OUT + 4
ODD_IN = FFN + PIECES_PER_SWIGLU
ODD_OUT = ODD_IN + 24
MOE = ODD_OUT + 8
EVEN_ORDER = [2, 3, 4, 1, 0]
ODD_CHUNKS = 12
FFN_EVENTS = T * STEPS

TURN_X, TURN_MIX, TURN_X1, TURN_X2, TURN_O, TURN_X3 = 0, 4, 8, 12, 16, 24
TURN_BANKS = ([4, 5, 6, 7] + [2, 3, 6, 7] + [2, 3, 6, 7] + [0, 1, 2, 3]
              + [0, 1, 2, 3, 0, 1, 2, 3] + [2, 3, 5, 6])

C_IDENT, C_PRECEDES, C_ONES, C_SLOT, C_CAUSAL, C_REV, C_ITEM = 0, 128, 256, 384, 512, 640, 648
C_WIDTH = 664
SCORE_COLS = P + SEQ

VEC = dict(ln1=0, ln2=1, gn=2, oln1=3, oln2=4)


def constants():
    table = np.zeros((P, C_WIDTH), np.float32)
    i = np.arange(P)
    table[:, C_IDENT:C_IDENT + P] = np.eye(P)
    table[:, C_PRECEDES:C_PRECEDES + P] = i[:, None] < i[None, :]
    table[:, C_ONES:C_ONES + P] = 1.0
    table[:, C_SLOT:C_SLOT + P] = i[None, :]
    table[:, C_CAUSAL:C_CAUSAL + P] = i[:, None] <= i[None, :]
    table[:, C_REV:C_REV + EXPERTS] = EXPERTS - np.arange(EXPERTS)[None, :]
    table[:, C_ITEM:C_ITEM + ITEMS] = np.arange(ITEMS)[None, :]
    slopes = (2.0 ** (-8.0 * np.arange(1, HEADS + 1) / HEADS)).astype(np.float32)
    q = np.concatenate([np.repeat(i[:, None], P, 1), P + np.repeat(i[:, None], SEQ, 1)], 1)
    k = np.concatenate([np.arange(P), np.arange(SEQ)])[None, :]
    alibi = np.stack([np.where(q >= k, -s * (q - k).astype(np.float32), np.float32(-1e30)) for s in slopes], 1)
    rate = np.log1p(-(2.0 ** (-5.0 - np.arange(RET_HEADS))))
    kk = np.concatenate([np.repeat(i[:, None], SEQ, 1), P + np.repeat(i[:, None], P, 1)], 1)
    qq = np.concatenate([np.arange(SEQ), P + np.arange(P)])[None, :]
    decay = np.stack([np.where(qq >= kk, np.exp(r * np.maximum(qq - kk, 0)) * 256.0 ** -0.5, 0.0) for r in rate], 1)
    return table, alibi.astype(np.float32), decay.astype(np.float32)


def o_block(b):
    return (b + 8) % 16


def plus(base, n):
    return base + n if not (isinstance(base, int) and base == 0) else n


class Chain:

    def __init__(self, eng, sem):
        self.eng, self.sem, self.n = eng, sem, 0

    def link(self, ins):
        self.n += 1
        ins.then_inc(self.sem, 1)
        self.eng.wait_ge(self.sem, self.n)


def hybrid_trunk(nc, a, out):
    with ExitStack() as ctx:
        place = [16512]

        def sb(name, shape, dt=F32, at=None):
            size = 4 * int(np.prod(shape[1:]))
            if at is None:
                at = place[0]
                place[0] += (size + 31) // 32 * 32
            return nc.alloc_sbuf_tensor_at(name, shape, dt, offset=at)

        def region(size):
            at = place[0]
            place[0] += size
            return at

        def sem(name):
            return ctx.enter_context(nc.semaphore(name))

        psum = [ctx.enter_context(nc.psum_tensor(f"bank{i}", [P, COLS], F32)) for i in range(8)]

        raw = sb("raw", [P, RAW_SLOTS, PIECE])
        w_hi = sb("w_hi", [P, SPLIT_SLOTS, PIECE], F32R)
        w_lo = sb("w_lo", [P, SPLIT_SLOTS, PIECE], F32R)
        xt_at = region(2 * 16 * SEQ * 4)
        xt_hi = sb("xt_hi", [P, 16, SEQ], F32R, at=xt_at)
        xt_lo = sb("xt_lo", [P, 16, SEQ], F32R, at=xt_at + 16 * SEQ * 4)
        x = sb("x", [P, T, D])
        table = sb("table", [P, C_WIDTH])
        vec = sb("vec", [P, 2048])
        bias = sb("bias", [P, HEADS, SCORE_COLS])
        ident = table[:, C_IDENT:C_IDENT + P]
        small = sb("small", [P, 160])
        stats = sb("stats", [P, 8, 6])

        upper = xt_at + 8 * SEQ * 4
        v_gain = sb("v_gain", [P, 512], at=upper)
        v_bias = sb("v_bias", [P, 512], at=upper + 2048)
        gate_w = sb("gate_w", [P, GROUPS, P], at=upper + 4096)
        lam_in = sb("lam_in", [P, 4, DH], at=upper + 6144)
        sub_gain = sb("sub_gain", [P, P], at=upper + 7168)
        b_s = sb("b_s", [P, GROUPS], at=upper + 7680)
        work = region(49152)
        mix = sb("mix", [P, T, D], at=work)
        qT = sb("qT", [P, HEADS, SEQ], at=work + 8192)
        kT = sb("kT", [P, HEADS, SEQ], at=work + 12288)
        va = sb("va", [P, T, 512], at=work + 16384)
        u_act = sb("u_act", [P, T, 512], at=work + 20480)
        v_act = sb("v_act", [P, T, 512], at=work + 24576)
        q_nat = sb("q_nat", [P, T, 512], at=work + 28672)
        k_nat = sb("k_nat", [P, T, 512], at=work + 32768)
        prob = sb("prob", [P, 2, 2, SCORE_COLS], at=work + 36864)
        attn = sb("attn", [P, 2, SCORE_COLS], at=work + 43008)
        attnT = sb("attnT", [P, 2, SCORE_COLS], at=work + 46080)
        r_v = sb("r_v", [P, T, 2048], at=work)
        r_g = sb("r_g", [P, T, 2048], at=work + 16384)
        r_qT = sb("r_qT", [P, KB, SEQ], at=work + 32768)
        r_kT = sb("r_kT", [P, KB, SEQ], at=work + 40960)
        qk_nat = sb("qk_nat", [P, 2, T, 512], at=upper)
        spare = region(5120)
        decayed = sb("decayed", [P, 2, SCORE_COLS], at=spare)
        o_norm = sb("o_norm", [P, RET_V], at=spare + 3072)
        silu = sb("silu", [P, T, COLS], at=work)
        g = sb("g", [P, T, COLS], at=work + 4096)
        gT_hi = sb("gT_hi", [P, FB, SEQ], F32R, at=work + 8192)
        gT_lo = sb("gT_lo", [P, FB, SEQ], F32R, at=work + 12288)
        acc = sb("acc", [P, T, D], at=work + 16384)
        slot_hi = sb("slot_hi", [P, KB, P], F32R, at=work + 32768)
        slot_lo = sb("slot_lo", [P, KB, P], F32R, at=work + 36864)
        y_hi = sb("y_hi", [P, D], F32R, at=work + 40960)
        y_lo = sb("y_lo", [P, D], F32R, at=work + 45056)
        pick = sb("pick", [P, T, P], at=spare)
        pickT = sb("pickT", [P, SEQ], F32R, at=spare + 1024)
        x3T = sb("x3T", [P, KB, SEQ], at=xt_at)
        wr = sb("wr", [P, KB, EXPERTS], at=spare + 2560)
        rb = sb("rb", [P, EXPERTS], at=spare + 2816)
        slot_no = sb("slot_no", [P, T, ITEMS], at=spare + 2848)
        gate = sb("gate", [P, T, ITEMS], at=spare + 2976)
        own_slot = sb("own_slot", [P, T, 1])
        plan_f = sb("plan_f", [P, 6, 32], at=spare + 3104)
        plan = sb("plan", [P, 2, ITEMS + 2], I32, at=spare + 3872)
        route = sb("route", [P, 10, T, EXPERTS], at=spare + 4096)
        order = sb("order", [P, ITEMS, ITEMS], at=xt_at)
        plan_g = sb("plan_g", [P, 2, ITEMS + 2], at=xt_at + 1024)
        assert place[0] <= nc.sbuf_usable_end

        def cols(first, n):
            return small[:, first:first + n]

        lam_dot, lam_exp, neg_lam = cols(0, 2), cols(2, 2), cols(4, 1)
        mean_var = small[:, 8:24].rearrange("p (n two) -> p n two", two=2)
        var_eps, std, rstd = cols(24, 8), cols(32, 8), cols(40, 8)
        top, neg_top, total, scale = (small[:, 48 + 8 * i:56 + 8 * i].rearrange("p (b n) -> p b n", b=2)
                                      for i in range(4))
        sub_ss, sub_std = cols(80, 8), cols(88, 8)
        ret_mv = small[:, 96:104].rearrange("p (n two) -> p n two", two=2)
        ret_var, ret_std, ret_rstd = cols(104, 4), cols(108, 4), cols(112, 4)
        peak1, peak2, best, share1, share2, gap, odds = (cols(116 + 2 * i, 2) for i in range(7))

        landed = [sem(f"piece_landed{i}") for i in range(RAW_SLOTS)]
        hi_ready = sem("hi_ready")
        lo_ready = sem("lo_ready")
        tile_summed = sem("tile_summed")
        piece_used = sem("piece_used")
        x_landed = [sem(f"x{t}_landed") for t in range(T)]
        table_landed, bias_landed = sem("table_landed"), sem("bias_landed")
        gating_landed, decay_landed, router_landed = sem("gating_landed"), sem("decay_landed"), sem("router_landed")
        vec_landed = [sem(f"vec_landed_{n}") for n in VEC]
        x_ready = sem("x_ready")
        turned = sem("turned")
        xt_hi_ready, xt_lo_ready = sem("xt_hi_ready"), sem("xt_lo_ready")
        lin_read = sem("lin_read")
        qk_turned, qT_ready, kT_ready = sem("qk_turned"), sem("qT_ready"), sem("kT_ready")
        scores_done, scores_read = sem("scores_done"), sem("scores_read")
        top_ready, exp_ready = sem("top_ready"), sem("exp_ready")
        attn_ready, attn_turned, attnT_ready = sem("attn_ready"), sem("attn_turned"), sem("attnT_ready")
        pv_done = sem("pv_done")
        lam_dotted, lam_exped = sem("lam_dotted"), sem("lam_exped")
        var_ready, std_ready = sem("var_ready"), sem("std_ready")
        v_ready, gating_done, mix_ready = sem("v_ready"), sem("gating_done"), sem("mix_ready")
        ret_turned, ret_T_ready = sem("ret_turned"), sem("ret_T_ready")
        ret_scores, ret_decayed, ret_out, o_ready = sem("ret_scores"), sem("ret_decayed"), sem("ret_out"), sem("o_ready")
        bias_used = sem("bias_used")
        silu_ready, g_ready, g_turned = sem("silu_ready"), sem("g_ready"), sem("g_turned")
        gT_hi_ready, gT_lo_ready = sem("gT_hi_ready"), sem("gT_lo_ready")
        x3T_by_act, x3T_by_dve, logits_done = sem("x3T_by_act"), sem("x3T_by_dve"), sem("logits_done")
        gap_ready, odds_ready = sem("gap_ready"), sem("odds_ready")
        mask_ready, places_done, plan_ready = sem("mask_ready"), sem("places_done"), sem("plan_ready")
        slots_known = sem("slots_known")
        slot_copied, pick_begun = sem("slot_copied"), sem("pick_begun")
        pick_ready, gathered, pick_turned = sem("pick_ready"), sem("gathered"), sem("pick_turned")
        slot_hi_ready, slot_lo_ready, pickT_ready = sem("slot_hi_ready"), sem("slot_lo_ready"), sem("pickT_ready")
        y_hi_ready, y_lo_ready, scattered, added = sem("y_hi_ready"), sem("y_lo_ready"), sem("scattered"), sem("added")
        vector_step = sem("vector_step")
        stored = sem("stored")

        block = ctx.enter_context(nc.Block())

        def col_piece(w, half, first_col):
            return w[half * 4 * P:(half + 1) * 4 * P, bass.ds(first_col, COLS)].rearrange("(k p) n -> p k n", p=P)

        def row_piece(w, pair):
            return w[bass.ds(pair * 2 * P, 2 * P), :].rearrange("(k p) n -> p k n", p=P)

        @block.sync
        def _(sp):
            def load(n, base, src, k, c):
                if not isinstance(base, int) or n >= RAW_SLOTS:
                    sp.wait_ge(lo_ready, plus(base, n + 1 - RAW_SLOTS))
                dst = raw[:, n % RAW_SLOTS, :].rearrange("p (k c) -> p k c", k=k)
                sp.dma_start(dst, src).then_inc(landed[n % RAW_SLOTS], 16)

            def swiglu_stream(n, base, w1, w3, w2):
                def up(n, base, j):
                    for i, w in enumerate((w3, w1)):
                        for half in range(2):
                            load(n + 2 * i + half, base, col_piece(w, half, j * COLS), 4, COLS)

                def down(n, base, j):
                    for half in range(2):
                        load(n + half, base, row_piece(w2, j * 2 + half), 2, D)

                up(n, base, 0)
                with sp.Fori(1, STEPS) as j:
                    here = base + (j - 1) * 6
                    up(n + 4, here, j)
                    down(n + 8, here, j - 1)
                down(n + 4 + 6 * (STEPS - 1), base, STEPS - 1)

            for t in range(T):
                sp.dma_start(x[:, t, :], a["x"][t * P:(t + 1) * P, :]).then_inc(x_landed[t], 16)
            for i, c in enumerate(EVEN_ORDER):
                for half in range(2):
                    load(EVEN_IN + 2 * i + half, 0, col_piece(a["even_w_in"], half, c * COLS), 4, COLS)
            for pair in range(4):
                load(EVEN_OUT + pair, 0, row_piece(a["even_w_o"], pair), 2, D)
            swiglu_stream(FFN, 0, a["ffn_w1"], a["ffn_w3"], a["ffn_w2"])
            for c in range(ODD_CHUNKS):
                for half in range(2):
                    load(ODD_IN + 2 * c + half, 0, col_piece(a["odd_w_in"], half, c * COLS), 4, COLS)
            for pair in range(8):
                load(ODD_OUT + pair, 0, row_piece(a["odd_w_o"], pair), 2, D)

            def expert_stream(k, e):
                w1, w3, w2 = (a[n][bass.ds(e, 1), :, :].rearrange("o k n -> (o k) n")
                              for n in ("moe_w1", "moe_w3", "moe_w2"))
                swiglu_stream(MOE, k * PIECES_PER_SWIGLU, w1, w3, w2)

            with sp.Fori(0, EXPERTS) as k:
                expert_stream(k, k)
            sp.wait_ge(plan_ready, 1)
            runs_n = sp.value_load(plan[0:1, 0, 0:1], min_val=EXPERTS, max_val=TURNS)
            with sp.Fori(EXPERTS, TURNS) as k:
                e = sp.value_load(plan[0:1, 1, bass.ds(k + 1, 1)], min_val=0, max_val=EXPERTS - 1)
                with sp.If(runs_n > k):
                    expert_stream(k, e)

            for t in range(T):
                sp.wait_ge(x_ready, 3 * T + t + 1)
                sp.dma_start(out[t * P:(t + 1) * P, :], acc[:, t, :]).then_inc(stored, 16)
            sp.wait_ge(stored, 16 * T)

        @block.gpsimd
        def _(pool):
            pool.wait_ge(landed[1], 16)
            pool.dma_start(bias[:], a["alibi"]).then_inc(bias_landed, 16)
            for i, n in enumerate(("even_lam_q1", "even_lam_k1", "even_lam_q2", "even_lam_k2")):
                pool.dma_start(lam_in[:, i, :], a[n].partition_broadcast(P)).then_inc(gating_landed, 16)
            pool.dma_start(v_gain[:], a["even_v_ln_g"].partition_broadcast(P)).then_inc(gating_landed, 16)
            pool.dma_start(v_bias[:], a["even_v_ln_b"].partition_broadcast(P)).then_inc(gating_landed, 16)
            pool.dma_start(gate_w[:], a["even_w_s_t"]).then_inc(gating_landed, 16)
            pool.dma_start(b_s[:], a["even_b_s_t"]).then_inc(gating_landed, 16)
            pool.dma_start(sub_gain[:], a["even_subln_g"].partition_broadcast(P)).then_inc(gating_landed, 16)

            def norm_vectors(at, names, width):
                for i, n in enumerate(names):
                    pool.dma_start(vec[:, i * width:(i + 1) * width],
                                   a[n].partition_broadcast(P)).then_inc(vec_landed[at], 16)

            norm_vectors(0, ("even_ln1_g", "even_ln1_b"), D)
            pool.wait_ge(bias_used, 1)
            pool.dma_start(bias[:], a["decay"]).then_inc(decay_landed, 16)
            pool.wait_ge(x_ready, T)
            norm_vectors(1, ("even_ln2_g", "even_ln2_b"), D)
            pool.wait_ge(x_ready, 2 * T)
            norm_vectors(2, ("odd_gn_g",), 2048)
            pool.wait_ge(o_ready, RET_HEADS)
            norm_vectors(3, ("odd_ln1_g", "odd_ln1_b"), D)
            pool.dma_start(wr[:], a["router_w"].rearrange("(k p) e -> p k e", p=P)).then_inc(router_landed, 16)
            pool.dma_start(rb[:], a["router_b"].partition_broadcast(P)).then_inc(router_landed, 16)
            pool.wait_ge(x_ready, 3 * T)
            norm_vectors(4, ("odd_ln2_g", "odd_ln2_b"), D)

            def build_pick(k, item):
                pool.tensor_copy(own_slot[:], slot_no[:, :, bass.ds(item, 1)]).then_inc(slot_copied, 1)
                pool.wait_ge(slot_copied, plus(k, 1))
                pool.sem_inc(pick_begun, 1)
                for t in range(T):
                    last = pool.tensor_scalar(pick[:, t, :], table[:, C_SLOT:C_SLOT + P], own_slot[:, t, :],
                                              None, ALU.is_equal)
                last.then_inc(pick_ready, 1)

            pool.wait_ge(slots_known, 1)
            build_pick(0, 0)
            pool.wait_ge(plan_ready, 1)
            runs_n = pool.value_load(plan[0:1, 0, 0:1], min_val=EXPERTS, max_val=TURNS)
            with pool.Fori(0, TURNS) as k:
                with pool.If(runs_n > k):
                    pool.wait_ge(pick_turned, k + 1)
                    item = pool.value_load(plan[0:1, 0, bass.ds(k + 2, 1)], min_val=0, max_val=ITEMS - 1)
                    build_pick(k + 1, item)

        @block.tensor
        def _(pe):
            def split_product(acc, hi, lo, b_hi, b_lo, start, stop):
                pe.matmul(acc, hi, b_hi, start=start, stop=False)
                pe.matmul(acc, hi, b_lo, start=False, stop=False)
                return pe.matmul(acc, lo, b_hi, start=False, stop=stop)

            def col_product(n, base, half, banks, hi, lo):
                pe.wait_ge(lo_ready, plus(base, n + 1))
                s = n % SPLIT_SLOTS
                for k in range(4):
                    for t, bank in enumerate(banks):
                        last = split_product(psum[bank][:], hi[:, 4 * half + k, t * P:(t + 1) * P],
                                             lo[:, 4 * half + k, t * P:(t + 1) * P],
                                             w_hi[:, s, k * COLS:(k + 1) * COLS], w_lo[:, s, k * COLS:(k + 1) * COLS],
                                             start=(half == 0 and k == 0), stop=(half == 1 and k == 3))
                last.then_inc(piece_used, 1)

            def row_product(n, base, first_block, banks, hi, lo, start, stop):
                pe.wait_ge(lo_ready, plus(base, n + 1))
                s = n % SPLIT_SLOTS
                for t, pair in enumerate(banks):
                    for k in range(2):
                        for h, bank in enumerate(pair):
                            c = k * D + h * COLS
                            last = split_product(psum[bank][:], hi[:, first_block + k, t * P:(t + 1) * P],
                                                 lo[:, first_block + k, t * P:(t + 1) * P],
                                                 w_hi[:, s, c:c + COLS], w_lo[:, s, c:c + COLS],
                                                 start=(start and k == 0), stop=(stop and k == 1))
                    if stop and t == 0 and len(banks) == T:
                        last.then_inc(tile_summed, 1)
                last.then_inc(piece_used, 1)

            def turn(group, src, block0):
                bank = psum[TURN_BANKS[group]]
                for k in range(2):
                    for t in range(T):
                        c = (block0 + k) * P
                        last = pe.transpose(bank[:, k * SEQ + t * P:k * SEQ + (t + 1) * P], src[:, t, c:c + P], ident)
                last.then_inc(turned, 1)

            def turn_x(first_group, ready):
                for t in range(T):
                    pe.wait_ge(*ready(t))
                    for i in range(4):
                        bank = psum[TURN_BANKS[first_group + i]]
                        for k in range(2):
                            c = (2 * i + k) * P
                            last = pe.transpose(bank[:, k * SEQ + t * P:k * SEQ + (t + 1) * P], x[:, t, c:c + P], ident)
                        if t == T - 1:
                            last.then_inc(turned, 1)

            def halves_split(first_group):
                return lambda half: pe.wait_ge(xt_lo_ready, first_group + 2 * half + 2)

            def linear(n, number, banks, hold=2, blocks=None):
                if number >= hold:
                    pe.wait_ge(lin_read, number - hold + 1)
                for half in range(2):
                    if blocks:
                        blocks(half)
                    col_product(n + half, 0, half, banks, xt_hi, xt_lo)

            def nothing():
                pass

            def swiglu(n, base, events, hi, lo, tiles, y_banks, after_first=nothing, after_turn=nothing,
                       before_last=nothing, blocks=None):
                h3, h1 = [0, 1][:tiles], [2, 3][:tiles] if tiles == 2 else [1]

                def up(n, base, done, blocks=None):
                    for half in range(2):
                        if blocks:
                            blocks(half)
                        col_product(n + half, base, half, h3, hi, lo)
                    if done is not None:
                        pe.wait_ge(gT_lo_ready, done)
                    for half in range(2):
                        col_product(n + 2 + half, base, half, h1, hi, lo)

                def down(n, base, start, stop):
                    for half in range(2):
                        row_product(n + half, base, 2 * half, y_banks, gT_hi, gT_lo,
                                    start and half == 0, stop and half == 1)

                def turn_g(done):
                    for t in range(tiles):
                        pe.wait_ge(g_ready, plus(done, t + 1))
                        for b in range(FB):
                            last = pe.transpose(psum[h1[t]][:, b * P:(b + 1) * P], g[:, t, b * P:(b + 1) * P], ident)
                        last.then_inc(g_turned, 1)

                up(n, base, None, blocks)
                after_first()
                turn_g(events)
                after_turn()
                up(n + 4, base, plus(events, tiles))
                down(n + 8, base, True, False)
                turn_g(plus(events, tiles))
                with pe.Fori(2, STEPS) as j:
                    here = base + (j - 1) * 6
                    now = events + j * tiles
                    up(n + 4, here, now)
                    down(n + 8, here, False, False)
                    turn_g(now)
                before_last()
                pe.wait_ge(gT_lo_ready, plus(events, STEPS * tiles))
                down(n + 4 + 6 * (STEPS - 1), base, False, True)

            pe.wait_ge(table_landed, 16)
            turn_x(TURN_X, lambda t: (x_landed[t], 16))

            linear(EVEN_IN, 0, [0, 1], blocks=halves_split(TURN_X))
            linear(EVEN_IN + 2, 1, [2, 3])
            linear(EVEN_IN + 4, 2, [0, 1])
            pe.wait_ge(lin_read, 2)
            for i, nat in enumerate((q_nat, k_nat)):
                for h in range(HEADS):
                    for t in range(T):
                        c = (h % 2) * SEQ + t * P
                        last = pe.transpose(psum[4 + 2 * i + h // 2][:, c:c + P], nat[:, t, h * P:(h + 1) * P], ident)
                last.then_inc(qk_turned, 1)
            def scores(h):
                if h >= 2:
                    pe.wait_ge(scores_read, h - 1)
                for c in range(2):
                    bank = psum[4 + 2 * (h % 2) + c]
                    rows = slice(c * DH, (c + 1) * DH)
                    pe.matmul(bank[:, 0:P], qT[rows, h, 0:P], kT[rows, h, 0:P], start=True, stop=True)
                    last = pe.matmul(bank[:, P:SCORE_COLS], qT[rows, h, P:SEQ], kT[rows, h, :], start=True, stop=True)
                last.then_inc(scores_done, 1)

            pe.wait_ge(lin_read, 2)
            col_product(EVEN_IN + 6, 0, 0, [2, 3], xt_hi, xt_lo)
            pe.wait_ge(qT_ready, 1)
            pe.wait_ge(kT_ready, 1)
            scores(0)
            scores(1)
            col_product(EVEN_IN + 7, 0, 1, [2, 3], xt_hi, xt_lo)
            pe.wait_ge(lin_read, 3)
            col_product(EVEN_IN + 8, 0, 0, [0, 1], xt_hi, xt_lo)
            scores(2)
            scores(3)
            def turn_attn(h):
                pe.wait_ge(attn_ready, h + 1)
                if h < 2:
                    pe.wait_ge(lin_read, 4)
                for b in range(3):
                    last = pe.transpose(psum[2 + h % 2][:, b * P:(b + 1) * P], attn[:, h % 2, b * P:(b + 1) * P], ident)
                last.then_inc(attn_turned, 1)

            def values(h):
                pe.wait_ge(attnT_ready, h + 1)
                c = slice(h * P, (h + 1) * P)
                pe.matmul(psum[6][:, c], attnT[:, h % 2, 0:P], va[:, 0, c], start=True, stop=True)
                pe.matmul(psum[7][:, c], attnT[:, h % 2, P:2 * P], va[:, 0, c], start=True, stop=False)
                pe.matmul(psum[7][:, c], attnT[:, h % 2, 2 * P:3 * P], va[:, 1, c],
                          start=False, stop=True).then_inc(pv_done, 1)

            turn_attn(0)
            turn_attn(1)
            col_product(EVEN_IN + 9, 0, 1, [0, 1], xt_hi, xt_lo)
            pe.wait_ge(scores_read, HEADS)
            values(0)
            values(1)
            turn_attn(2)
            values(2)
            turn_attn(3)
            values(3)
            pe.wait_ge(v_ready, 1)
            pe.wait_ge(scores_read, 3)
            for t in range(T):
                for gr in range(GROUPS):
                    last = pe.matmul(psum[4 + t][:, gr * P:(gr + 1) * P], gate_w[:, gr, :],
                                     v_act[:, t, gr * P:(gr + 1) * P], start=True, stop=True)
            last.then_inc(gating_done, 1)
            for pair in range(4):
                if pair % 2 == 0:
                    pe.wait_ge(mix_ready, pair // 2 + 1)
                    turn(TURN_MIX + pair, mix, 2 * pair)
                    turn(TURN_MIX + pair + 1, mix, 2 * pair + 2)
                pe.wait_ge(xt_lo_ready, TURN_MIX + pair + 1)
                row_product(EVEN_OUT + pair, 0, 2 * pair, [[0, 1], [4, 5]], xt_hi, xt_lo, pair == 0, pair == 3)

            turn_x(TURN_X1, lambda t: (x_ready, 0 * T + t + 1))
            swiglu(FFN, 0, 0, xt_hi, xt_lo, T, [[4, 5], [6, 7]], blocks=halves_split(TURN_X1))

            turn_x(TURN_X2, lambda t: (x_ready, 1 * T + t + 1))

            def turn_qk(c):
                pe.wait_ge(lin_read, 5 + c + 1)
                if c >= 2:
                    pe.wait_ge(ret_T_ready, c - 1)
                for b in range(4):
                    for t in range(T):
                        k = (b % 2) * SEQ + t * P
                        last = pe.transpose(psum[4 + 2 * (c % 2) + b // 2][:, k:k + P],
                                            qk_nat[:, c % 2, t, b * P:(b + 1) * P], ident)
                last.then_inc(ret_turned, 1)

            def ret_head_scores(h):
                if h:
                    pe.wait_ge(ret_decayed, h)
                for tile, c0, c1 in ((0, 0, SEQ), (1, SEQ, SCORE_COLS)):
                    for k in range(2):
                        last = pe.matmul(psum[4][:, c0:c1], r_kT[:, 2 * h + k, tile * P:(tile + 1) * P],
                                         r_qT[:, 2 * h + k, tile * P:SEQ], start=(k == 0), stop=(k == 1))
                last.then_inc(ret_scores, 1)

            def ret_head_values(h):
                pe.wait_ge(ret_decayed, h + 1)
                if h:
                    pe.wait_ge(o_ready, h)
                s, v = decayed[:, h % 2, :], slice(h * RET_V, (h + 1) * RET_V)
                pe.matmul(psum[5][:], s[:, 0:P], r_v[:, 0, v], start=True, stop=True)
                pe.matmul(psum[6][:], s[:, P:SEQ], r_v[:, 0, v], start=True, stop=False)
                pe.matmul(psum[6][:], s[:, SEQ:SCORE_COLS], r_v[:, 1, v],
                          start=False, stop=True).then_inc(ret_out, 1)

            def turn_o(h):
                pe.wait_ge(o_ready, h + 1)
                for i in range(2):
                    turn(TURN_O + 2 * h + i, r_g, 4 * h + 2 * i)

            for c in range(ODD_CHUNKS):
                if c in (10, 11):
                    pe.wait_ge(xt_lo_ready, TURN_O + 2 * (c - 9))
                if c == 1:
                    pe.wait_ge(xt_lo_ready, TURN_X2 + 4)
                linear(ODD_IN + 2 * c, 5 + c, [[0, 1], [2, 3]][c % 2],
                       blocks=halves_split(TURN_X2) if c == 0 else None)
                if 1 <= c <= 4:
                    turn_qk(c - 1)
                if c >= 8:
                    h = c - 8
                    if h == 0:
                        pe.wait_ge(ret_T_ready, 4)
                        pe.wait_ge(lin_read, 5 + 8)
                    ret_head_scores(h)
                    if h:
                        turn_o(h - 1)
                    ret_head_values(h)
            odd_banks = [[0, 1], [4, 7]]
            for pair in range(8):
                if pair == 6:
                    pe.wait_ge(lin_read, 5 + ODD_CHUNKS)
                    turn_o(3)
                pe.wait_ge(xt_lo_ready, TURN_O + min(max(pair + 1, 6), 8))
                row_product(ODD_OUT + pair, 0, o_block(2 * pair), odd_banks, xt_hi, xt_lo, pair == 0, pair == 7)

            turn_x(TURN_X3, lambda t: (x_ready, 2 * T + t + 1))
            pe.wait_ge(router_landed, 32)
            for k in range(KB):
                if k % 2 == 0:
                    pe.wait_ge((x3T_by_act, x3T_by_dve)[k // 2 % 2], k // 4 + 1)
                for t in range(T):
                    last = pe.matmul(psum[4 * t][:, 0:EXPERTS], x3T[:, k, t * P:(t + 1) * P], wr[:, k, :],
                                     start=(k == 0), stop=(k == KB - 1))
            last.then_inc(logits_done, 1)
            pe.wait_ge(mask_ready, 1)
            masks = route[:, 8, :, :]
            precedes, ones = table[:, C_PRECEDES:C_PRECEDES + P], table[:, C_ONES:C_ONES + P]
            pe.matmul(psum[1][:, 0:EXPERTS], precedes, masks[:, 0, :], start=True, stop=True)
            pe.matmul(psum[1][:, EXPERTS:2 * EXPERTS], ones, masks[:, 0, :], start=True, stop=False)
            pe.matmul(psum[1][:, EXPERTS:2 * EXPERTS], precedes, masks[:, 1, :], start=False, stop=True)
            for t in range(T):
                last = pe.matmul(psum[1][:, 2 * EXPERTS:3 * EXPERTS], ones, masks[:, t, :], start=(t == 0), stop=(t == 1))
            last.then_inc(places_done, 1)

            def gather(k):
                pe.wait_ge(pick_ready, plus(k, 1))
                for b in range(KB):
                    for t in range(T):
                        last = pe.matmul(psum[2 + b // 4][:, (b % 4) * P:(b % 4 + 1) * P], x[:, t, b * P:(b + 1) * P],
                                         pick[:, t, :], start=(t == 0), stop=(t == T - 1))
                last.then_inc(gathered, 1)

            def scatter(k):
                pe.wait_ge(y_lo_ready, plus(k, 1))
                for t in range(T):
                    for h in range(2):
                        bank = psum[(2, 3, 6, 7)[2 * t + h]]
                        c = slice(h * COLS, (h + 1) * COLS)
                        pe.matmul(bank[:], pickT[:, t * P:(t + 1) * P], y_hi[:, c], start=True, stop=False)
                        pe.matmul(bank[:], pickT[:, t * P:(t + 1) * P], y_lo[:, c],
                                  start=False, stop=True).then_inc(scattered, 1)

            gather(0)
            pe.wait_ge(plan_ready, 1)
            runs_n = pe.value_load(plan[0:1, 0, 0:1], min_val=EXPERTS, max_val=TURNS)
            with pe.Fori(0, TURNS) as k:
                with pe.If(runs_n > k):
                    def scatter_and_turn():
                        scatter(k)
                        pe.wait_ge(g_ready, k * STEPS + (FFN_EVENTS + 1))
                        for t in range(T):
                            last = pe.transpose(psum[0][:, t * P:(t + 1) * P], pick[:, t, :], ident)
                        last.then_inc(pick_turned, 1)

                    def gather_next():
                        pe.wait_ge(added, k * 4 + 2)
                        with pe.If(runs_n > k + 1):
                            gather(k + 1)

                    pe.wait_ge(slot_lo_ready, k + 1)
                    swiglu(MOE, k * PIECES_PER_SWIGLU, k * STEPS + FFN_EVENTS, slot_hi, slot_lo, 1, [[4, 5]],
                           after_first=scatter_and_turn, before_last=gather_next,
                           after_turn=lambda: pe.wait_ge(pickT_ready, k + 1))
            scatter(runs_n)

        @block.scalar
        def _(act):
            done = [0]

            def hi_part(n, base, landings):
                act.wait_ge(landed[n % RAW_SLOTS], plus(landings, 16 * (n // RAW_SLOTS + 1)))
                if not isinstance(base, int) or n >= SPLIT_SLOTS:
                    act.wait_ge(piece_used, plus(base, n + 1 - SPLIT_SLOTS))
                act.activation(w_hi[:, n % SPLIT_SLOTS, :], raw[:, n % RAW_SLOTS, :], ACT.Copy).then_inc(hi_ready, 1)

            def split_to(n):
                while done[0] < n:
                    hi_part(done[0], 0, 0)
                    done[0] += 1

            def turned_hi(group, blk, banks=None):
                act.wait_ge(turned, group + 1)
                act.activation(xt_hi[:, blk:blk + 2, :], psum[TURN_BANKS[group]][:].rearrange("p (k s) -> p k s", k=2),
                               ACT.Copy).then_inc(xt_hi_ready, 1)

            def read_linear(last_piece, banks, dst, fn=ACT.Copy):
                split_to(last_piece + 2)
                act.wait_ge(piece_used, last_piece + 1)
                for t in range(T):
                    last = act.activation(dst[t], psum[banks[t]][:], fn)
                last.then_inc(lin_read, 1)

            def root(number, dst, src):
                act.wait_ge(var_ready, number)
                act.activation(dst, src, ACT.Sqrt).then_inc(std_ready, 1)

            def norm(first_root):
                for t in range(T):
                    root(first_root + t, std[:, t:t + 1], var_eps[:, t:t + 1])

            def nothing():
                pass

            def swiglu(n, base, landings, events, tiles, split_before, after_first=nothing):
                h1 = [2, 3] if tiles == 2 else [1]

                def silu_step(n, base, now):
                    act.wait_ge(piece_used, plus(base, n + 1))
                    for t in range(tiles):
                        act.activation(silu[:, t, :], psum[h1[t]][:], ACT.Silu).then_inc(silu_ready, 1)

                def turned_g(now):
                    for t in range(tiles):
                        act.wait_ge(g_turned, plus(now, t + 1))
                        act.activation(gT_hi[:, :, t * P:(t + 1) * P], psum[h1[t]][:].rearrange("p (b s) -> p b s", b=FB),
                                       ACT.Copy).then_inc(gT_hi_ready, 1)

                for i in range(split_before, 6):
                    hi_part(n + i, base, landings)
                silu_step(n + 3, base, events)
                after_first()
                turned_g(events)
                with act.Fori(1, STEPS) as j:
                    here = base + (j - 1) * 6
                    land = landings + (j - 1) * 16
                    now = events + j * tiles
                    for i in range(2, 6):
                        hi_part(n + 4 + i, here, land)
                    silu_step(n + 7, here, now)
                    for i in range(6, 8):
                        hi_part(n + 4 + i, here, land)
                    turned_g(now)

            act.dma_start(table[:], a["table"]).then_inc(table_landed, 16)
            for i in range(2):
                turned_hi(TURN_X + i, 2 * i)
            split_to(1)
            for i in range(2, 4):
                turned_hi(TURN_X + i, 2 * i)

            read_linear(EVEN_IN + 1, [0, 1], [q_nat[:, t, :] for t in range(T)])
            read_linear(EVEN_IN + 3, [2, 3], [k_nat[:, t, :] for t in range(T)])
            read_linear(EVEN_IN + 5, [0, 1], [va[:, t, :] for t in range(T)])
            act.wait_ge(qk_turned, 1)
            for i in range(2):
                last = act.activation(qT[:, 2 * i:2 * i + 2, :], psum[4 + i][:].rearrange("p (h s) -> p h s", h=2), ACT.Copy)
            last.then_inc(qT_ready, 1)
            split_to(EVEN_IN + 9)

            def exps(h):
                act.wait_ge(top_ready, h + 1)
                b = h % 2
                for c in range(2):
                    for t, (c0, c1) in enumerate(((0, P), (P, SCORE_COLS))):
                        i = 2 * c + t
                        last = act.activation(prob[:, b, c, c0:c1], prob[:, b, c, c0:c1], ACT.Exp,
                                              bias=neg_top[:, b, i:i + 1], accum_out=total[:, b, i:i + 1])
                last.then_inc(exp_ready, 1)

            def turned_attn(h):
                act.wait_ge(attn_turned, h + 1)
                if h >= 2:
                    act.wait_ge(pv_done, h - 1)
                act.activation(attnT[:, h % 2, :], psum[2 + h % 2][:, 0:SCORE_COLS], ACT.Copy).then_inc(attnT_ready, 1)

            act.wait_ge(lam_dotted, 1)
            act.activation(lam_exp, lam_dot, ACT.Exp).then_inc(lam_exped, 1)
            exps(0)
            exps(1)
            read_linear(EVEN_IN + 7, [2, 3], [v_act[:, t, :] for t in range(T)], ACT.Gelu)
            split_to(EVEN_IN + 10)
            turned_attn(0)
            exps(2)
            turned_attn(1)
            exps(3)
            root(1, std, var_eps)
            for h in (2, 3):
                turned_attn(h)
            read_linear(EVEN_IN + 9, [0, 1], [u_act[:, t, :] for t in range(T)], ACT.Gelu)
            split_to(EVEN_OUT + 3)
            for i in range(2):
                turned_hi(TURN_MIX + i, 2 * i)
            root(2, sub_std, sub_ss)
            split_to(EVEN_OUT + 4)
            for i in range(2, 4):
                turned_hi(TURN_MIX + i, 2 * i)
            split_to(EVEN_OUT + 6)
            norm(3)
            for i in range(4):
                turned_hi(TURN_X1 + i, 2 * i)

            swiglu(FFN, 0, 0, 0, T, done[0] - FFN)
            done[0] = ODD_IN
            split_to(ODD_IN + 2)
            norm(5)
            for i in range(4):
                turned_hi(TURN_X2 + i, 2 * i)

            for c in range(ODD_CHUNKS):
                banks = [[0, 1], [2, 3]][c % 2]
                if c < 4:
                    if c >= 2:
                        act.wait_ge(ret_turned, c - 1)
                    dst, fn = [qk_nat[:, c % 2, t, :] for t in range(T)], ACT.Copy
                elif c < 8:
                    dst, fn = [r_v[:, t, (c - 4) * COLS:(c - 3) * COLS] for t in range(T)], ACT.Copy
                else:
                    dst, fn = [r_g[:, t, (c - 8) * COLS:(c - 7) * COLS] for t in range(T)], ACT.Silu
                if c >= 9:
                    split_to(ODD_IN + 2 * c + 2)
                    root(7 + c - 9, ret_std[:, 0:T], ret_var[:, 0:T])
                read_linear(ODD_IN + 2 * c + 1, banks, dst, fn)
                if c >= 9:
                    split_to(ODD_IN + 2 * c + 4)
                    for i in range(2):
                        turned_hi(TURN_O + 2 * (c - 9) + i, o_block(4 * (c - 9) + 2 * i))
            split_to(ODD_OUT + 3)
            root(10, ret_std[:, 0:T], ret_var[:, 0:T])
            split_to(ODD_OUT + 8)
            for i in range(2):
                turned_hi(TURN_O + 6 + i, o_block(12 + 2 * i))
            norm(11)

            for i in (0, 2):
                act.wait_ge(turned, TURN_X3 + i + 1)
                act.activation(x3T[:, 2 * i:2 * i + 2, :], psum[TURN_BANKS[TURN_X3 + i]][:].rearrange("p (k s) -> p k s", k=2),
                               ACT.Copy).then_inc(x3T_by_act, 1)
            split_to(MOE + 2)
            act.wait_ge(gap_ready, 1)
            act.activation(odds, gap, ACT.Exp).then_inc(odds_ready, 1)

            def slots_hi(k):
                act.wait_ge(gathered, plus(k, 1))
                for i in range(2):
                    last = act.activation(slot_hi[:, 4 * i:4 * i + 4, :],
                                          psum[2 + i][:].rearrange("p (k s) -> p k s", k=4), ACT.Copy)
                last.then_inc(slot_hi_ready, 1)

            def rows_hi(k):
                for h in range(2):
                    act.activation(y_hi[:, h * COLS:(h + 1) * COLS], psum[4 + h][:], ACT.Copy).then_inc(y_hi_ready, 1)

            slots_hi(0)
            act.wait_ge(plan_ready, 1)
            runs_n = act.value_load(plan[0:1, 0, 0:1], min_val=EXPERTS, max_val=TURNS)
            with act.Fori(0, TURNS) as k:
                with act.If(runs_n > k):
                    pieces = k * PIECES_PER_SWIGLU

                    def turned_pick():
                        act.wait_ge(pick_turned, k + 1)
                        act.activation(pickT[:], psum[0][:, 0:SEQ], ACT.Copy).then_inc(pickT_ready, 1)

                    act.wait_ge(piece_used, pieces + MOE)
                    rows_hi(k)
                    swiglu(MOE, pieces, k * (16 * STEPS), k * STEPS + FFN_EVENTS, 1, 2, after_first=turned_pick)
                    with act.If(runs_n > k + 1):
                        slots_hi(k + 1)
                        for i in range(2):
                            hi_part(MOE + PIECES_PER_SWIGLU + i, pieces, k * (16 * STEPS))
            act.wait_ge(piece_used, runs_n * PIECES_PER_SWIGLU + MOE)
            rows_hi(runs_n)
            norm(13)

        @block.vector
        def _(dve):
            own = Chain(dve, vector_step)
            done = [0]

            def lo_part(n, base):
                dve.wait_ge(hi_ready, plus(base, n + 1))
                dve.tensor_tensor(w_lo[:, n % SPLIT_SLOTS, :], raw[:, n % RAW_SLOTS, :],
                                  w_hi[:, n % SPLIT_SLOTS, :].bitcast(F32), ALU.subtract).then_inc(lo_ready, 1)

            def split_to(n):
                while done[0] < n:
                    lo_part(done[0], 0)
                    done[0] += 1

            def turned_lo(group, blk):
                dve.wait_ge(xt_hi_ready, group + 1)
                dve.tensor_tensor(xt_lo[:, blk:blk + 2, :], psum[TURN_BANKS[group]][:].rearrange("p (k s) -> p k s", k=2),
                                  xt_hi[:, blk:blk + 2, :].bitcast(F32), ALU.subtract).then_inc(xt_lo_ready, 1)

            def inverse_root(number, dst, src, from_act):
                own.link(dve.tensor_scalar(src, src, EPS, None, ALU.add))
                dve.sem_inc(var_ready, 1)
                dve.wait_ge(std_ready, number)
                own.link(dve.reciprocal(dst, from_act))

            def layer_norm(number, root_no, last_piece, banks):
                rows = x if banks else acc
                for t in range(T):
                    if banks and t == 0:
                        split_to(last_piece + 1)
                        dve.wait_ge(tile_summed, number + 1)
                    if banks and t == 1:
                        dve.wait_ge(piece_used, last_piece + 1)
                    if banks:
                        for h in range(2):
                            part = rows[:, t, h * COLS:(h + 1) * COLS]
                            ins = dve.scalar_tensor_tensor(out=part, in0=part, scalar=ALPHA, in1=psum[banks[t][h]][:],
                                                           op0=ALU.mult, op1=ALU.add)
                        own.link(ins)
                    for h in range(2):
                        ins = dve.bn_stats(stats[:, 2 * t + h, :], rows[:, t, h * COLS:(h + 1) * COLS])
                    own.link(ins)
                    own.link(dve.bn_aggr(mean_var[:, t, :], stats[:, 2 * t:2 * t + 2, :]))
                    own.link(dve.tensor_scalar(var_eps[:, t:t + 1], mean_var[:, t, 1:2], EPS, None, ALU.add))
                    dve.sem_inc(var_ready, 1)
                    if t == 0:
                        dve.wait_ge(vec_landed[(0, 1, 3, 4)[number]], 32)
                    own.link(dve.scalar_tensor_tensor(out=rows[:, t, :], in0=rows[:, t, :], scalar=mean_var[:, t, 0:1],
                                                      in1=vec[:, 0:D], op0=ALU.subtract, op1=ALU.mult))
                    dve.wait_ge(std_ready, root_no + t)
                    own.link(dve.reciprocal(rstd[:, t:t + 1], std[:, t:t + 1]))
                    dve.scalar_tensor_tensor(out=rows[:, t, :], in0=rows[:, t, :], scalar=rstd[:, t:t + 1],
                                             in1=vec[:, D:2 * D], op0=ALU.mult, op1=ALU.add).then_inc(x_ready, 1)

            def nothing():
                pass

            def swiglu(n, base, events, tiles, split_before, after_first=nothing):
                h3, h1 = [0, 1][:tiles], [2, 3] if tiles == 2 else [1]

                def product(now):
                    for t in range(tiles):
                        dve.wait_ge(silu_ready, plus(now, t + 1))
                        dve.tensor_tensor(g[:, t, :], silu[:, t, :], psum[h3[t]][:], ALU.mult).then_inc(g_ready, 1)

                def turned_g(now):
                    for t in range(tiles):
                        dve.wait_ge(gT_hi_ready, plus(now, t + 1))
                        dve.tensor_tensor(gT_lo[:, :, t * P:(t + 1) * P], psum[h1[t]][:].rearrange("p (b s) -> p b s", b=FB),
                                          gT_hi[:, :, t * P:(t + 1) * P].bitcast(F32), ALU.subtract).then_inc(gT_lo_ready, 1)

                for i in range(split_before, 6):
                    lo_part(n + i, base)
                product(events)
                turned_g(events)
                after_first()
                with dve.Fori(1, STEPS) as j:
                    here = base + (j - 1) * 6
                    now = events + j * tiles
                    for i in range(2, 6):
                        lo_part(n + 4 + i, here)
                    product(now)
                    for i in range(6, 8):
                        lo_part(n + 4 + i, here)
                    turned_g(now)

            for i in range(2):
                turned_lo(TURN_X + i, 2 * i)
            split_to(1)
            for i in range(2, 4):
                turned_lo(TURN_X + i, 2 * i)
            split_to(EVEN_IN + 5)

            dve.wait_ge(gating_landed, 16 * 9)
            dve.wait_ge(table_landed, 16)
            for i in range(2):
                ins = dve.tensor_tensor_reduce(prob[:, 0, i, 0:DH], lam_in[:, 2 * i, :], lam_in[:, 2 * i + 1, :], 1.0, 0.0,
                                               ALU.mult, ALU.add, lam_dot[:, i:i + 1])
            own.link(ins)
            dve.sem_inc(lam_dotted, 1)
            for gr in range(GROUPS):
                ins = dve.tensor_tensor(gate_w[:, gr, :], gate_w[:, gr, :], table[:, C_CAUSAL:C_CAUSAL + P], ALU.mult)
            own.link(ins)
            own.link(dve.tensor_scalar(sub_gain[:], sub_gain[:], 1.0 - LAM_INIT, None, ALU.mult))
            split_to(EVEN_IN + 7)
            dve.wait_ge(qk_turned, 2)
            for i in range(2):
                ins = dve.tensor_copy(kT[:, 2 * i:2 * i + 2, :], psum[6 + i][:].rearrange("p (h s) -> p h s", h=2))
            ins.then_inc(kT_ready, 1)
            split_to(EVEN_IN + 8)

            def softmax_top(h):
                b = h % 2
                dve.wait_ge(scores_done, h + 1)
                for c in range(2):
                    ins = dve.scalar_tensor_tensor(out=prob[:, b, c, :], in0=psum[4 + 2 * b + c][:, 0:SCORE_COLS],
                                                   scalar=DH ** -0.5, in1=bias[:, h, :], op0=ALU.mult, op1=ALU.add)
                own.link(ins)
                dve.sem_inc(scores_read, 1)
                if h == HEADS - 1:
                    dve.sem_inc(bias_used, 1)
                for c in range(2):
                    for t, (c0, c1) in enumerate(((0, P), (P, SCORE_COLS))):
                        ins = dve.reduce_max(top[:, b, 2 * c + t:2 * c + t + 1], prob[:, b, c, c0:c1], AX_X)
                own.link(ins)
                dve.tensor_scalar(neg_top[:, b, :], top[:, b, :], -1.0, None, ALU.mult).then_inc(top_ready, 1)

            def softmax_combine(h):
                b = h % 2
                dve.wait_ge(exp_ready, h + 1)
                own.link(dve.reciprocal(scale[:, b, :], total[:, b, :]))
                own.link(dve.tensor_scalar(scale[:, b, 2:4], scale[:, b, 2:4], neg_lam, None, ALU.mult))
                for t, (c0, c1) in enumerate(((0, P), (P, SCORE_COLS))):
                    ins = dve.tensor_scalar(prob[:, b, 1, c0:c1], prob[:, b, 1, c0:c1], scale[:, b, 2 + t:3 + t],
                                            None, ALU.mult)
                own.link(ins)
                if h >= 2:
                    dve.wait_ge(attn_turned, h - 1)
                for t, (c0, c1) in enumerate(((0, P), (P, SCORE_COLS))):
                    ins = dve.scalar_tensor_tensor(out=attn[:, b, c0:c1], in0=prob[:, b, 0, c0:c1],
                                                   scalar=scale[:, b, t:t + 1], in1=prob[:, b, 1, c0:c1],
                                                   op0=ALU.mult, op1=ALU.add)
                own.link(ins)
                dve.sem_inc(attn_ready, 1)

            dve.wait_ge(bias_landed, 16)
            softmax_top(0)
            softmax_top(1)
            split_to(EVEN_IN + 9)
            dve.wait_ge(lam_exped, 1)
            own.link(dve.tensor_tensor(neg_lam, lam_exp[:, 1:2], lam_exp[:, 0:1], ALU.subtract))
            own.link(dve.tensor_scalar(neg_lam, neg_lam, -LAM_INIT, None, ALU.add))
            softmax_combine(0)
            split_to(EVEN_IN + 10)
            softmax_combine(1)
            softmax_top(2)
            softmax_top(3)
            dve.wait_ge(lin_read, 4)
            for t in range(T):
                for gr in range(GROUPS):
                    ins = dve.bn_stats(stats[:, 4 * t + gr, :], v_act[:, t, gr * P:(gr + 1) * P])
            own.link(ins)
            for i in range(8):
                ins = dve.bn_aggr(mean_var[:, i, :], stats[:, i:i + 1, :])
            own.link(ins)
            own.link(dve.tensor_scalar(var_eps, mean_var[:, :, 1], EPS, None, ALU.add))
            dve.sem_inc(var_ready, 1)
            softmax_combine(2)
            softmax_combine(3)
            dve.wait_ge(std_ready, 1)
            own.link(dve.reciprocal(rstd, std))
            for t in range(T):
                for gr in range(GROUPS):
                    c = slice(gr * P, (gr + 1) * P)
                    ins = dve.scalar_tensor_tensor(out=v_act[:, t, c], in0=v_act[:, t, c],
                                                   scalar=mean_var[:, 4 * t + gr, 0:1], in1=v_gain[:, c],
                                                   op0=ALU.subtract, op1=ALU.mult)
            own.link(ins)
            for t in range(T):
                for gr in range(GROUPS):
                    i = 4 * t + gr
                    c = slice(gr * P, (gr + 1) * P)
                    ins = dve.scalar_tensor_tensor(out=v_act[:, t, c], in0=v_act[:, t, c], scalar=rstd[:, i:i + 1],
                                                   in1=v_bias[:, c], op0=ALU.mult, op1=ALU.add)
            own.link(ins)
            dve.sem_inc(v_ready, 1)
            split_to(EVEN_OUT + 1)
            dve.wait_ge(pv_done, HEADS)
            for t in range(T):
                ins = dve.tensor_copy(va[:, t, :], psum[6 + t][:])
            own.link(ins)
            dve.wait_ge(gating_done, 1)
            dve.wait_ge(lin_read, 5)
            for t in range(T):
                for gr in range(GROUPS):
                    c = slice(gr * P, (gr + 1) * P)
                    ins = dve.scalar_tensor_tensor(out=mix[:, t, c], in0=psum[4 + t][:, c], scalar=b_s[:, gr:gr + 1],
                                                   in1=u_act[:, t, c], op0=ALU.add, op1=ALU.mult)
            own.link(ins)
            dve.sem_inc(mix_ready, 1)
            split_to(EVEN_OUT + 2)
            for i in range(2):
                turned_lo(TURN_MIX + i, 2 * i)
            split_to(EVEN_OUT + 3)
            for t in range(T):
                ins = dve.tensor_tensor(q_nat[:, t, :], va[:, t, :], va[:, t, :], ALU.mult)
            own.link(ins)
            own.link(dve.tensor_reduce(sub_ss, q_nat[:].rearrange("p t (h d) -> p (t h) d", h=HEADS), AX_X, ALU.add))
            own.link(dve.tensor_scalar(sub_ss, sub_ss, 1.0 / P, EPS, ALU.mult, ALU.add))
            dve.sem_inc(var_ready, 1)
            dve.wait_ge(std_ready, 2)
            own.link(dve.reciprocal(sub_ss, sub_std))
            for t in range(T):
                for h in range(HEADS):
                    c = slice(h * P, (h + 1) * P)
                    ins = dve.scalar_tensor_tensor(out=mix[:, t, 512 + h * P:512 + (h + 1) * P], in0=va[:, t, c],
                                                   scalar=sub_ss[:, 4 * t + h:4 * t + h + 1], in1=sub_gain[:],
                                                   op0=ALU.mult, op1=ALU.mult)
            own.link(ins)
            dve.sem_inc(mix_ready, 1)
            for i in range(2, 4):
                turned_lo(TURN_MIX + i, 2 * i)
            split_to(EVEN_OUT + 4)
            layer_norm(0, 3, EVEN_OUT + 3, [[0, 1], [4, 5]])
            split_to(EVEN_OUT + 5)
            for i in range(2):
                turned_lo(TURN_X1 + i, 2 * i)
            split_to(EVEN_OUT + 6)
            for i in range(2, 4):
                turned_lo(TURN_X1 + i, 2 * i)

            swiglu(FFN, 0, 0, T, done[0] - FFN)
            done[0] = ODD_IN
            layer_norm(1, 5, ODD_IN - 1, [[4, 5], [6, 7]])
            split_to(ODD_IN + 1)
            for i in range(2):
                turned_lo(TURN_X2 + i, 2 * i)
            split_to(ODD_IN + 2)
            for i in range(2, 4):
                turned_lo(TURN_X2 + i, 2 * i)

            def turned_qk(c):
                dve.wait_ge(ret_turned, c + 1)
                dst = (r_qT, r_kT)[c // 2]
                for i in range(2):
                    b = 4 * (c % 2) + 2 * i
                    ins = dve.tensor_copy(dst[:, b:b + 2, :], psum[4 + 2 * (c % 2) + i][:].rearrange("p (k s) -> p k s", k=2))
                ins.then_inc(ret_T_ready, 1)

            def decay(h):
                dve.wait_ge(ret_scores, h + 1)
                dve.tensor_tensor(decayed[:, h % 2, :], psum[4][:, 0:SCORE_COLS], bias[:, h, :],
                                  ALU.mult).then_inc(ret_decayed, 1)

            def head_norm(h):
                dve.wait_ge(ret_out, h + 1)
                for t in range(T):
                    ins = dve.bn_stats(stats[:, t, :], psum[5 + t][:])
                own.link(ins)
                for t in range(T):
                    ins = dve.bn_aggr(ret_mv[:, t, :], stats[:, t:t + 1, :])
                own.link(ins)
                own.link(dve.tensor_copy(ret_var[:, 0:T], ret_mv[:, 0:T, 1]))
                inverse_root(7 + h, ret_rstd[:, 0:T], ret_var[:, 0:T], ret_std[:, 0:T])
                dve.wait_ge(vec_landed[2], 16)
                dve.wait_ge(lin_read, 5 + 9 + h)
                for t in range(T):
                    own.link(dve.scalar_tensor_tensor(out=o_norm[:], in0=psum[5 + t][:], scalar=ret_mv[:, t, 0:1],
                                                      in1=vec[:, h * RET_V:(h + 1) * RET_V],
                                                      op0=ALU.subtract, op1=ALU.mult))
                    part = r_g[:, t, h * RET_V:(h + 1) * RET_V]
                    own.link(dve.scalar_tensor_tensor(out=part, in0=o_norm[:], scalar=ret_rstd[:, t:t + 1], in1=part,
                                                      op0=ALU.mult, op1=ALU.mult))
                dve.sem_inc(o_ready, 1)
    
            for c in range(ODD_CHUNKS):
                split_to(ODD_IN + 2 * c + (3 if c < 9 else 2))
                if 1 <= c <= 4:
                    turned_qk(c - 1)
                if c == 8:
                    dve.wait_ge(decay_landed, 16)
                if c >= 9:
                    head_norm(c - 9)
                    split_to(ODD_IN + 2 * c + 3)
                    decay(c - 8)
                    for i in range(2):
                        turned_lo(TURN_O + 2 * (c - 9) + i, o_block(4 * (c - 9) + 2 * i))
                if c == 8:
                    decay(0)
            split_to(ODD_OUT + 2)
            head_norm(3)
            split_to(ODD_OUT + 8)
            for i in range(2):
                turned_lo(TURN_O + 6 + i, o_block(12 + 2 * i))
            layer_norm(2, 11, ODD_OUT + 7, [[0, 1], [4, 7]])

            for i in (1, 3):
                dve.wait_ge(turned, TURN_X3 + i + 1)
                dve.tensor_copy(x3T[:, 2 * i:2 * i + 2, :], psum[TURN_BANKS[TURN_X3 + i]][:].rearrange(
                    "p (k s) -> p k s", k=2)).then_inc(x3T_by_dve, 1)
            for t in range(T):
                ins = dve.tensor_scalar(acc[:, t, :], x[:, t, :], ALPHA, None, ALU.mult)
            own.link(ins)
            split_to(MOE + 1)
            logits, is_top, rank, first, rest, is_next, second, gates, mask, spare_r = (route[:, i, :, :] for i in range(10))
            rev = table[:, C_REV:C_REV + EXPERTS]
            dve.wait_ge(logits_done, 1)
            dve.wait_ge(router_landed, 32)
            for t in range(T):
                ins = dve.tensor_tensor(logits[:, t, :], psum[4 * t][:, 0:EXPERTS], rb[:], ALU.add)
            own.link(ins)

            def pick_first(values, peak, equal, chosen):
                own.link(dve.reduce_max(peak, values, AX_X))
                for t in range(T):
                    ins = dve.scalar_tensor_tensor(out=equal[:, t, :], in0=values[:, t, :], scalar=peak[:, t:t + 1],
                                                   in1=rev, op0=ALU.is_equal, op1=ALU.mult)
                own.link(ins)
                own.link(dve.reduce_max(best, equal, AX_X))
                for t in range(T):
                    ins = dve.tensor_scalar(chosen[:, t, :], equal[:, t, :], best[:, t:t + 1], None, ALU.is_equal)
                own.link(ins)

            pick_first(logits, peak1, is_top, first)
            own.link(dve.scalar_tensor_tensor(out=rest, in0=first, scalar=LOWEST, in1=logits, op0=ALU.mult, op1=ALU.add))
            pick_first(rest, peak2, is_next, second)
            own.link(dve.tensor_tensor(mask, first, second, ALU.add))
            dve.sem_inc(mask_ready, 1)
            own.link(dve.tensor_tensor(gap, peak2, peak1, ALU.subtract))
            dve.sem_inc(gap_ready, 1)
            own.link(dve.tensor_scalar(spare_r, mask, -NOT_CHOSEN, NOT_CHOSEN, ALU.mult, ALU.add))
            dve.wait_ge(places_done, 1)
            places = psum[1][:, 0:T * EXPERTS].rearrange("p (t e) -> p t e", t=T)
            own.link(dve.tensor_tensor(slot_no[:, :, 0:EXPERTS], spare_r, places, ALU.add))
            own.link(dve.tensor_scalar(slot_no[:, :, EXPERTS:ITEMS], slot_no[:, :, 0:EXPERTS], float(-P), None, ALU.add))
            dve.sem_inc(slots_known, 1)
            split_to(MOE + 2)
            own.link(dve.memset(plan_f[:], 0.0))
            for i in range(TILES):
                ins = dve.tensor_scalar(plan_f[:, 0, 16 + i * EXPERTS:16 + (i + 1) * EXPERTS],
                                        psum[1][:, 2 * EXPERTS:3 * EXPERTS], float(i * P - (i == 0)), None, ALU.is_gt)
            own.link(ins)
            for i in range(4):
                own.link(dve.tensor_tensor(plan_f[:, i + 1, 16:32], plan_f[:, i, 16:32],
                                           plan_f[:, i, 16 - 2 ** i:32 - 2 ** i], ALU.add))
            own.link(dve.tensor_tensor(plan_f[:, 5, 16:32], plan_f[:, 4, 16:32], plan_f[:, 0, 16:32], ALU.subtract))
            numbers = table[:, C_ITEM:C_ITEM + ITEMS]
            by_turn = [P, ITEMS, ITEMS]
            own.link(dve.tensor_tensor(order[:], plan_f[:, 5:6, 16:32].broadcast_to(by_turn),
                                       numbers.unsqueeze(2).broadcast_to(by_turn), ALU.is_equal))
            own.link(dve.tensor_tensor(order[:], order[:], plan_f[:, 0:1, 16:32].broadcast_to(by_turn), ALU.mult))
            own.link(dve.memset(plan_g[:], 0.0))
            own.link(dve.tensor_tensor(order[:], order[:], numbers.unsqueeze(1).broadcast_to(by_turn), ALU.mult))
            own.link(dve.tensor_reduce(plan_g[:, 0, 1:ITEMS + 1], order[:], AX_X, ALU.add))
            own.link(dve.tensor_scalar(plan_g[:, 1, :], plan_g[:, 0, :], EXPERTS - 0.5, -float(EXPERTS), ALU.is_gt, ALU.mult))
            own.link(dve.tensor_tensor(plan_g[:, 1, :], plan_g[:, 1, :], plan_g[:, 0, :], ALU.add))
            own.link(dve.tensor_copy(plan_g[:, 0, 0:1], plan_f[:, 4, 31:32]))
            own.link(dve.tensor_copy(plan[:], plan_g[:]))
            own.link(dve.memset(pickT[:].bitcast(F32), 0.0))
            dve.sem_inc(plan_ready, 1)
            dve.wait_ge(odds_ready, 1)
            own.link(dve.tensor_scalar(share1, odds, 1.0, None, ALU.add))
            own.link(dve.reciprocal(share1, share1))
            own.link(dve.tensor_tensor(share2, odds, share1, ALU.mult))
            for t in range(T):
                ins = dve.tensor_scalar(spare_r[:, t, :], second[:, t, :], share2[:, t:t + 1], None, ALU.mult)
            own.link(ins)
            for t in range(T):
                ins = dve.scalar_tensor_tensor(out=gates[:, t, :], in0=first[:, t, :], scalar=share1[:, t:t + 1],
                                               in1=spare_r[:, t, :], op0=ALU.mult, op1=ALU.add)
            own.link(ins)
            for i in range(TILES):
                ins = dve.tensor_copy(gate[:, :, i * EXPERTS:(i + 1) * EXPERTS], gates)
            own.link(ins)

            def slots_lo(k):
                dve.wait_ge(slot_hi_ready, plus(k, 1))
                for i in range(2):
                    ins = dve.tensor_tensor(slot_lo[:, 4 * i:4 * i + 4, :], psum[2 + i][:].rearrange("p (k s) -> p k s", k=4),
                                            slot_hi[:, 4 * i:4 * i + 4, :].bitcast(F32), ALU.subtract)
                ins.then_inc(slot_lo_ready, 1)

            def rows_lo(k):
                for h in range(2):
                    c = slice(h * COLS, (h + 1) * COLS)
                    dve.wait_ge(y_hi_ready, k * 2 + (h + 1))
                    ins = dve.tensor_tensor(y_lo[:, c], psum[4 + h][:], y_hi[:, c].bitcast(F32), ALU.subtract)
                ins.then_inc(y_lo_ready, 1)

            def add_rows(k, item):
                for t in range(T):
                    for h in range(2):
                        part = acc[:, t, h * COLS:(h + 1) * COLS]
                        dve.wait_ge(scattered, k * 4 + (2 * t + h + 1))
                        dve.scalar_tensor_tensor(out=part, in0=psum[(2, 3, 6, 7)[2 * t + h]][:],
                                                 scalar=gate[:, t, bass.ds(item, 1)], in1=part,
                                                 op0=ALU.mult, op1=ALU.add).then_inc(added, 1)

            slots_lo(0)
            runs_n = dve.value_load(plan[0:1, 0, 0:1], min_val=EXPERTS, max_val=TURNS)
            with dve.Fori(0, TURNS) as k:
                with dve.If(runs_n > k):
                    last_item = dve.value_load(plan[0:1, 0, bass.ds(k, 1)], min_val=0, max_val=ITEMS - 1)
                    pieces = k * PIECES_PER_SWIGLU
                    rows_lo(k)
                    swiglu(MOE, pieces, k * STEPS + FFN_EVENTS, 1, 2, after_first=lambda: add_rows(k, last_item))
                    with dve.If(runs_n > k + 1):
                        slots_lo(k + 1)
                        for i in range(2):
                            lo_part(MOE + PIECES_PER_SWIGLU + i, pieces)
            rows_lo(runs_n)
            last_item = dve.value_load(plan[0:1, 0, bass.ds(runs_n, 1)], min_val=0, max_val=ITEMS - 1)
            add_rows(runs_n, last_item)
            dve.wait_ge(added, runs_n * 4 + 4)
            own.link(dve.memset(stats[:], 0.0))
            layer_norm(3, 13, None, None)


def kernel(**inputs):
    import numpy as _np
    import concourse.bacc as _bacc
    from concourse import mybir as _mybir
    from concourse.bass_utils import run_bass_kernel_spmd as _run

    def layer(name):
        return _np.asarray(inputs[name])[0]

    table, alibi, decay = constants()
    arrays = {"x": _np.asarray(inputs["x"])[0], "table": table, "alibi": alibi, "decay": decay}
    for name in ("even_w_in", "even_w_o", "ffn_w1", "ffn_w3", "ffn_w2", "odd_w_in", "odd_w_o", "router_w",
                 "moe_w1", "moe_w3", "moe_w2"):
        arrays[name] = layer(name)
    for name in ("even_v_ln_g", "even_v_ln_b", "even_lam_q1", "even_lam_k1", "even_lam_q2", "even_lam_k2",
                 "even_subln_g", "even_ln1_g", "even_ln1_b", "even_ln2_g", "even_ln2_b", "odd_gn_g",
                 "odd_ln1_g", "odd_ln1_b", "router_b", "odd_ln2_g", "odd_ln2_b"):
        arrays[name] = layer(name).reshape(-1)
    arrays["even_w_s_t"] = layer("even_w_s").transpose(2, 0, 1)
    arrays["even_b_s_t"] = layer("even_b_s").T

    nc = _bacc.Bacc("TRN2", target_bir_lowering=False, num_devices=1)
    aps, feed = {}, {}
    for name, value in arrays.items():
        value = _np.ascontiguousarray(value)
        feed[f"in_{name}"] = value
        aps[name] = nc.dram_tensor(f"in_{name}", value.shape, _mybir.dt.from_np(value.dtype), kind="ExternalInput").ap()
    out = nc.dram_tensor("out_x", (SEQ, D), F32, kind="ExternalOutput").ap()
    hybrid_trunk(nc, aps, out)
    r = _run(nc, [feed], core_ids=[0])
    return r.results[0]["out_x"].reshape(1, SEQ, D)
```
